# Optimizing a Trainium2 kernel written in Bass

```python
import math
import jax, jax.numpy as jnp
from jax import lax
import numpy as np

D_MODEL = 1024
BATCH = 1
SEQ = 512
DEPTH = 2

CONV_WIDTH = D_MODEL
CONV_K = 3
HEAD_DIM = 64
V_HEAD_DIM = 2 * HEAD_DIM
N_DIFF_HEADS = D_MODEL // V_HEAD_DIM
QK_WIDTH = N_DIFF_HEADS * 2 * HEAD_DIM
ATTN_WIDTH = N_DIFF_HEADS * V_HEAD_DIM
ROT_DIM = HEAD_DIM // 4
ROPE_THETA = 500000.0
Q_BLOCK = 128
D_FF = ((8 * D_MODEL // 3 + 255) // 256) * 256
NORM_EPS = 1e-6
N_BRANCHES = 2
IN_WIDTH = 3 * CONV_WIDTH + 2 * QK_WIDTH + ATTN_WIDTH + N_BRANCHES * D_MODEL

kernel_name = "hybrid_gated_conv_diffattn_macaron_encoder"

def rmsnorm(x, w):
    xf = x.astype(jnp.float32)
    y = xf * lax.rsqrt(jnp.mean(xf * xf, axis=-1, keepdims=True) + NORM_EPS)
    return (y * w.astype(jnp.float32)).astype(x.dtype)

def swiglu(x, w13, w2):
    g, u = jnp.split(x @ w13, 2, axis=-1)
    return (jax.nn.silu(g) * u) @ w2

def rope_tables(seq_len):
    pos = jnp.arange(seq_len, dtype=jnp.float32)
    inv = ROPE_THETA ** (-jnp.arange(0, ROT_DIM, 2, dtype=jnp.float32) / ROT_DIM)
    ang = pos[:, None] * inv[None, :]
    return jnp.cos(ang), jnp.sin(ang)

def apply_partial_rope(t, cos, sin):
    c = cos[None, :, None, None, :].astype(t.dtype)
    s = sin[None, :, None, None, :].astype(t.dtype)
    half = ROT_DIM // 2
    t1 = t[..., :half]
    t2 = t[..., half:ROT_DIM]
    return jnp.concatenate([t1 * c - t2 * s, t2 * c + t1 * s, t[..., ROT_DIM:]], axis=-1)

def short_conv(u, w):
    up = jnp.pad(u, ((0, 0), (1, 1), (0, 0)))
    s = u.shape[1]
    return up[:, 0:s] * w[0] + up[:, 1:s + 1] * w[1] + up[:, 2:s + 2] * w[2]

def diff_attention(q, k, v, lam, lam_init, subln_w):
    b, s = q.shape[0], q.shape[1]
    nb = s // Q_BLOCK
    qb = q.reshape(b, nb, Q_BLOCK, N_DIFF_HEADS, 2, HEAD_DIM).transpose(1, 0, 3, 4, 2, 5)
    kt = k.transpose(0, 2, 3, 1, 4)
    vt = v.transpose(0, 2, 1, 3)
    scale = HEAD_DIM ** -0.5

    def block(qblk):
        sc = jnp.einsum('bhcqd,bhckd->bhcqk', qblk, kt).astype(jnp.float32) * scale
        p = jax.nn.softmax(sc, axis=-1)
        a = p[:, :, 0] - lam * p[:, :, 1]
        return jnp.einsum('bhqk,bhkd->bhqd', a.astype(vt.dtype), vt)

    o = lax.map(block, qb)
    o = o.transpose(1, 0, 3, 2, 4).reshape(b, s, N_DIFF_HEADS, V_HEAD_DIM)
    o = rmsnorm(o, subln_w) * (1.0 - lam_init)
    return o.reshape(b, s, ATTN_WIDTH)

def token_mixer(h, w_in, b_gate, conv_w, w_conv_out, w_attn_out, lam_vec, subln_w, w_o,
                lam_init, cos, sin):
    b, s = h.shape[0], h.shape[1]
    z = h @ w_in
    c0 = CONV_WIDTH
    q0 = 3 * c0
    idx = [c0, 2 * c0, q0, q0 + QK_WIDTH, q0 + 2 * QK_WIDTH, q0 + 2 * QK_WIDTH + ATTN_WIDTH]
    bg, cg, hc, q, k, v, gl = jnp.split(z, idx, axis=-1)
    y_conv = (bg * short_conv(cg * hc, conv_w)) @ w_conv_out
    q = apply_partial_rope(q.reshape(b, s, N_DIFF_HEADS, 2, HEAD_DIM), cos, sin)
    k = apply_partial_rope(k.reshape(b, s, N_DIFF_HEADS, 2, HEAD_DIM), cos, sin)
    v = v.reshape(b, s, N_DIFF_HEADS, V_HEAD_DIM)
    lv = lam_vec.astype(jnp.float32)
    lam = jnp.exp(jnp.sum(lv[0] * lv[1])) - jnp.exp(jnp.sum(lv[2] * lv[3])) + lam_init
    y_attn = diff_attention(q, k, v, lam, lam_init, subln_w) @ w_attn_out
    g_conv, g_attn = jnp.split(jax.nn.sigmoid(gl + b_gate), 2, axis=-1)
    return (g_conv * y_conv + g_attn * y_attn) @ w_o

def setup_inputs(seed: int = 0) -> dict:
    key = jax.random.key(seed)
    ks = jax.random.split(key, 14)
    nrm = jax.random.normal
    D = D_MODEL
    return {
        "x": nrm(ks[0], (BATCH, SEQ, D), jnp.float32),
        "w_in": nrm(ks[1], (DEPTH, D, IN_WIDTH), jnp.float32) * D ** -0.5,
        "b_gate": nrm(ks[2], (DEPTH, N_BRANCHES * D), jnp.float32) * 0.01,
        "conv_w": nrm(ks[3], (DEPTH, CONV_K, CONV_WIDTH), jnp.float32) * CONV_K ** -0.5,
        "w_conv_out": nrm(ks[4], (DEPTH, CONV_WIDTH, D), jnp.float32) * CONV_WIDTH ** -0.5,
        "w_attn_out": nrm(ks[5], (DEPTH, ATTN_WIDTH, D), jnp.float32) * ATTN_WIDTH ** -0.5,
        "lam_vec": nrm(ks[6], (DEPTH, 4, HEAD_DIM), jnp.float32) * 0.1,
        "subln_w": 1.0 + 0.02 * nrm(ks[7], (DEPTH, V_HEAD_DIM), jnp.float32),
        "w_o": nrm(ks[8], (DEPTH, D, D), jnp.float32) * D ** -0.5,
        "ffn1_w13": nrm(ks[9], (DEPTH, D, 2 * D_FF), jnp.float32) * D ** -0.5,
        "ffn1_w2": nrm(ks[10], (DEPTH, D_FF, D), jnp.float32) * D_FF ** -0.5,
        "ffn2_w13": nrm(ks[11], (DEPTH, D, 2 * D_FF), jnp.float32) * D ** -0.5,
        "ffn2_w2": nrm(ks[12], (DEPTH, D_FF, D), jnp.float32) * D_FF ** -0.5,
        "norm_w": 1.0 + 0.02 * nrm(ks[13], (DEPTH, 6, D), jnp.float32),
    }

def reference(x, w_in, b_gate, conv_w, w_conv_out, w_attn_out, lam_vec, subln_w, w_o,
              ffn1_w13, ffn1_w2, ffn2_w13, ffn2_w2, norm_w):
    cos, sin = rope_tables(x.shape[1])
    for l in range(DEPTH):
        nw = norm_w[l]
        lam_init = 0.8 - 0.6 * math.exp(-0.3 * l)
        x = x + 0.5 * rmsnorm(swiglu(rmsnorm(x, nw[0]), ffn1_w13[l], ffn1_w2[l]), nw[1])
        m = token_mixer(rmsnorm(x, nw[2]), w_in[l], b_gate[l], conv_w[l], w_conv_out[l],
                        w_attn_out[l], lam_vec[l], subln_w[l], w_o[l], lam_init, cos, sin)
        x = x + rmsnorm(m, nw[3])
        x = x + 0.5 * rmsnorm(swiglu(rmsnorm(x, nw[4]), ffn2_w13[l], ffn2_w2[l]), nw[5])
    return x


_drawn_inputs = setup_inputs


def setup_inputs(seed=0):
    import zlib

    import numpy as np

    out = dict(_drawn_inputs(seed))
    spreads = {}
    factors = {'b_gate': 8.0, 'subln_w': 3.994}
    for name, (base, spread) in spreads.items():
        noise = np.random.default_rng([zlib.crc32(name.encode()), seed]).standard_normal(out[name].shape)
        drawn = base * np.exp(spread * noise) if base else spread * noise
        out[name] = __import__('jax').numpy.asarray(drawn.astype(out[name].dtype))
    for name, factor in factors.items():
        out[name] = (out[name] * factor).astype(out[name].dtype)
    return out
```

```python
import math

import numpy as np
import concourse.bass as bass
from concourse import mybir
from contextlib import ExitStack

DEPTH = 2
D = 1024
T = 512
DFF = 2816
HEADS = 8
P = 128
KT = D // P
FT = DFF // P
UP = FT // 2
TT = T // P
HD = 64
EPS = 1e-6
SCALE = HD ** -0.5
STAGE = 2048

FFN = 2 * UP + UP
PAIRS = HEADS // 2
ATT = 6
MIX = ATT * PAIRS + 4 * 4 + 4
STAGES = 2 * FFN + MIX
M0 = FFN
GC0 = M0 + ATT * PAIRS
CO0 = GC0 + 4
AO0 = CO0 + 4
GA0 = AO0 + 4
WO0 = GA0 + 4
F20 = M0 + MIX
WIDE = 2 * 2 * UP + ATT * PAIRS + 8
RAW_CREDIT = 2
READ_CREDIT = 2
CREDIT = 1


def encoder_kernel(nc, xT, w_in, w_conv_out, w_attn_out, w_o, ffn1_w13, ffn1_w2, ffn2_w13, ffn2_w2,
                   norm_wT, b_gateT, conv_wT, sublnT, lam_vec, ropeC, ropeS, ident_in, lam_const, out):
    f32, f32r, i32 = mybir.dt.float32, mybir.dt.float32r, mybir.dt.int32
    ALU, ACT, AX = mybir.AluOpType, mybir.ActivationFunctionType, mybir.AxisListType
    ds = bass.ds

    with ExitStack() as ctx:
        def sb(name, shape, dt=f32):
            return ctx.enter_context(nc.sbuf_tensor(name, shape, dt))

        def sem(name):
            return ctx.enter_context(nc.semaphore(name))

        x = sb("x", [P, KT, T])
        xh = sb("xh", [P, KT, T], f32r)
        xl = sb("xl", [P, KT, T], f32r)
        yw = sb("yw", [P, KT, T])
        hid = sb("hid", [P, FT, T])
        raw = sb("raw", [P, 2, STAGE])
        wh = sb("wh", [P, 2, STAGE], f32r)
        wl = sb("wl", [P, 2, STAGE], f32r)
        jit = sb("jit", [P, 2, 2, 2, T], f32r)
        aT = jit[:, :, :, :, :].rearrange("p a b c t -> p a (b c) t")
        qh = sb("qh", [P, T], f32r)
        ql = sb("ql", [P, T], f32r)
        kh = sb("kh", [P, 2, T], f32r)
        kl = sb("kl", [P, 2, T], f32r)
        vh = sb("vh", [P, TT, P], f32r)
        vl = sb("vl", [P, TT, P], f32r)
        cosT = sb("cosT", [P, T])
        sinT = sb("sinT", [P, T])
        rpre = sb("rpre", [P, T])
        acc = sb("acc", [P, T])
        sq = sb("sq", [P, 2, T])
        diag = sb("diag", [P, TT, P])
        ones = sb("ones", [P, P])
        ident = sb("ident", [P, P])
        nw = sb("nw", [P, DEPTH, 6, KT])
        bg = sb("bg", [P, DEPTH, 2, KT])
        cw = sb("cw", [P, DEPTH, 3, KT])
        sub = sb("sub", [P, DEPTH])
        lamc = sb("lamc", [P, 2, DEPTH])
        nlam = sb("nlam", [P, DEPTH])
        lsum = sb("lsum", [P, 2 * DEPTH])
        lexp = sb("lexp", [P, 2 * DEPTH])
        rv = sb("rv", [P, TT])
        rt = sb("rt", [P, TT])
        ry = sb("ry", [P, TT])
        mx = sb("mx", [P, 2])
        nmx = sb("nmx", [P, 2, 2])
        psums = sb("psums", [P, 2, 2])
        rsum = sb("rsum", [P, 2])
        c1 = sb("c1", [P, 2])
        gz, th, uz = yw[:, 0:2, :], yw[:, 2:4, :], yw[:, 4:6, :]
        zq, zk, zv = yw[:, 0:2, :], yw[:, 2:4, :], yw[:, 4:6, :]
        pm = yw[:, 6:8, :]
        convb = hid[:, 19:21, :]
        att = hid[:, 16:18, :]
        shuf = hid[:, 18, :]
        cu = hid[:, 21, :]
        gatez = hid[:, 16:18, :]
        gateth = hid[:, 18:20, :]
        lamv = hid[:, 0, 0:DEPTH * 4 * HD]
        PS = ctx.enter_context(nc.psum_tensor("PS", [P, 8, T], f32))
        SC, TR, OB = 4, 6, 7

        consts_in, x_in, y_out = sem("consts_in"), sem("x_in"), sem("y_out")
        cleared, params = sem("cleared"), sem("params")
        lam_sum, lam_exp = sem("lam_sum"), sem("lam_exp")
        w_loaded = [sem("w_loaded0"), sem("w_loaded1")]
        w_hi, w_lo, w_used = sem("w_hi"), sem("w_lo"), sem("w_used")
        x_ready, x_hi, xw_ready = sem("x_ready"), sem("x_hi"), sem("xw_ready")
        sq_ready, acc_done = sem("sq_ready"), sem("acc_done")
        stat, diag_ready, wide, r_ready = sem("stat"), sem("diag_ready"), sem("wide"), sem("r_ready")
        wide_read = sem("wide_read")
        gz_ready, th_ready, h_ready = sem("gz_ready"), sem("th_ready"), sem("h_ready")
        y_ready = sem("y_ready")
        y_scaled, co_read, ao_read = sem("y_scaled"), sem("co_read"), sem("ao_read")
        z_ready, q_hi, qk_lo = sem("z_ready"), sem("q_hi"), sem("qk_lo")
        v_tr, v_hi, v_lo = sem("v_tr"), sem("v_hi"), sem("v_lo")
        s_ready, s_max, s_exp = sem("s_ready"), sem("s_max"), sem("s_exp")
        c_ready, p_scaled, a_ready = sem("c_ready"), sem("p_scaled"), sem("a_ready")
        a_tr, a_hi, a_lo = sem("a_tr"), sem("a_hi"), sem("a_lo")
        pv, o_sq, o_stat, o_diag, o_wide, o_done = (sem("pv"), sem("o_sq"), sem("o_stat"), sem("o_diag"),
                                                    sem("o_wide"), sem("o_done"))
        conv_done = sem("conv_done")
        gate_z, gate_th, m_ready = sem("gate_z"), sem("gate_th"), sem("m_ready")
        N_CONST = 10

        block = ctx.enter_context(nc.Block())

        @block.sync
        def _(sp):
            for k in range(KT):
                sp.dma_start(x[:, k, :], xT[k * P:(k + 1) * P, :]).then_inc(x_in, 16)

            def load(L, s, slot, src):
                sp.wait_ge(w_lo, L * STAGES + s + (RAW_CREDIT - 1))
                sp.dma_start(raw[:, slot, :].rearrange("p (k c) -> p k c", c=src.shape[-1]), src) \
                    .then_inc(w_loaded[slot], 16)

            def wide_src(w, L, col):
                return w[L, :, ds(col, 256)].rearrange("(k p) c -> p k c", p=P)

            def deep_src(w, L, row):
                return w[L, ds(row, 2 * P), :].rearrange("(k p) c -> p k c", p=P)

            def ffn(L, s0, w13, w2):
                a = s0 % 2
                with sp.Fori(0, UP) as i:
                    load(L, s0 + i * 2, a, wide_src(w13, L, i * 256))
                    load(L, s0 + i * 2 + 1, 1 - a, wide_src(w13, L, i * 256 + DFF))
                s1 = s0 + 2 * UP
                with sp.Fori(0, UP // 2) as i:
                    load(L, s1 + i * 2, a, deep_src(w2, L, i * 4 * P))
                    load(L, s1 + i * 2 + 1, 1 - a, deep_src(w2, L, i * 4 * P + 2 * P))
                load(L, s1 + UP - 1, a, deep_src(w2, L, (UP - 1) * 2 * P))

            def four(L, s0, src):
                for n in range(4):
                    load(L, s0 + n, (s0 + n) % 2, src(n))

            with sp.Fori(0, DEPTH) as L:
                ffn(L, 0, ffn1_w13, ffn1_w2)
                with sp.Fori(0, PAIRS) as i:
                    for n, first in enumerate((3 * D, 4 * D, 5 * D, 0, D, 2 * D)):
                        load(L, M0 + i * ATT + n, (M0 + n) % 2, wide_src(w_in, L, i * 256 + first))
                four(L, GC0, lambda n: wide_src(w_in, L, 6 * D + n * 256))
                four(L, CO0, lambda n: deep_src(w_conv_out, L, n * 2 * P))
                four(L, AO0, lambda n: deep_src(w_attn_out, L, n * 2 * P))
                four(L, GA0, lambda n: wide_src(w_in, L, 7 * D + n * 256))
                four(L, WO0, lambda n: deep_src(w_o, L, n * 2 * P))
                ffn(L, F20, ffn2_w13, ffn2_w2)
            for k in range(KT):
                sp.wait_ge(x_ready, DEPTH * 3 * KT - KT + k + 1 + CREDIT)
                sp.dma_start(out[k * P:(k + 1) * P, :], x[:, k, :]).then_inc(y_out, 16)
            sp.wait_ge(y_out, 16 * KT)

        @block.gpsimd
        def _(pool):
            pool.memset(ones[:, :], 1.0).then_inc(cleared, 1)
            for t in (kh, kl):
                pool.memset(t[:, :, :].bitcast(f32), 0.0).then_inc(cleared, 1)

            def sums(L, n):
                for k in range(1, KT - 1):
                    pool.wait_ge(sq_ready, L * (6 * KT) + n * KT + k + 1)
                    if k > 1:
                        pool.wait_ge(acc_done, L * 36 + n * 6 + k - 1)
                    pool.tensor_tensor(acc[:, :], acc[:, :], sq[:, k % 2, :], ALU.add).then_inc(acc_done, 1)

            with pool.Fori(0, DEPTH) as L:
                with pool.Fori(0, 6) as n:
                    sums(L, n)

        @block.scalar
        def _(act):
            for dst, src in ((nw, norm_wT), (bg, b_gateT), (cw, conv_wT), (sub, sublnT), (lamc, lam_const),
                             (cosT, ropeC), (sinT, ropeS), (ident, ident_in)):
                flat = dst[:, :] if len(dst.shape) == 2 else dst[:].rearrange(
                    "p a b -> p (a b)" if len(dst.shape) == 3 else "p a b c -> p (a b c)")
                act.dma_start(flat, src[:, :]).then_inc(consts_in, 16)
            act.dma_start(lamv, lam_vec.rearrange("l a d -> (l a d)").partition_broadcast(P)).then_inc(consts_in, 16)

            def split(L, s, slot, src=None, ready=(), first=False):
                act.wait_ge(w_loaded[slot], L * (8 * STAGES) + s * 8 + (16 - 8 * slot))
                if not first:
                    act.wait_ge(w_used, L * STAGES + s - 1)
                for q, v in ready:
                    act.wait_ge(q, v)
                if src is not None:
                    act.activation(jit[:, slot, 0, :, :], src, ACT.Copy)
                act.activation(wh[:, slot, :], raw[:, slot, :], ACT.Copy).then_inc(w_hi, 1)

            def square(L, n, k, src):
                if k >= 3:
                    act.wait_ge(acc_done, L * 36 + n * 6 + k - 2)
                act.activation(acc[:, :] if k == 0 else sq[:, k % 2, :], src, ACT.Square).then_inc(sq_ready, 1)

            def pre(L, n):
                for k in range(KT):
                    act.wait_ge(x_ready, L * (3 * KT) + ((n - 1) * KT + k + 1 if n else 0) + CREDIT)
                    act.activation(xh[:, k, :], x[:, k, :], ACT.Copy, scale=nw[:, ds(L, 1), 2 * n, k]).then_inc(x_hi, 1)
                    square(L, 2 * n, k, x[:, k, :])

            def rms(L, n):
                act.wait_ge(wide, L * 6 + 2 * n + 1)
                act.activation(rpre[:, :], PS[:, 5, :], ACT.Copy).then_inc(r_ready, 1)

            def post(L, n):
                y0 = (0, 3 * KT, 4 * KT)[n]
                for m in range(KT):
                    act.wait_ge(y_ready, L * (5 * KT) + y0 + m + 1)
                    square(L, 2 * n + 1, m, PS[:, m, :])
                    act.activation(yw[:, m, :], PS[:, m, :], ACT.Copy, scale=nw[:, ds(L, 1), 2 * n + 1, m]) \
                       .then_inc(y_scaled, 1)

            def ffn(L, w, s0, n):
                a = s0 % 2
                G = (L * 2 + w) * UP
                pre(L, n)

                def step(i, s, last, first=False):
                    def up_src(ii):
                        return hid[:, ds(ii * 2, 2), :]
                    split(L, s + 2, a, None if not last else up_src(0), [(h_ready, G + 1)] if last else ())
                    if first:
                        rms(L, n)
                    act.wait_ge(gz_ready, G + i + 1)
                    act.activation(th, gz, ACT.Tanh, scale=0.5).then_inc(th_ready, 1)
                    split(L, s + 3, 1 - a, None if not last else up_src(1), [(h_ready, G + 2)] if last else ())

                step(0, s0, False, first=True)
                with act.Fori(1, UP - 1) as i:
                    step(i, s0 + i * 2, False)
                step(UP - 1, s0 + 2 * (UP - 1), True)
                s1 = s0 + 2 * UP
                with act.Fori(0, (UP - 3) // 2) as i:
                    split(L, s1 + i * 2 + 2, a, hid[:, ds(i * 4 + 4, 2), :], [(h_ready, G + i * 2 + 3)])
                    split(L, s1 + i * 2 + 3, 1 - a, hid[:, ds(i * 4 + 6, 2), :], [(h_ready, G + i * 2 + 4)])
                split(L, s1 + UP - 1, a, hid[:, FT - 2:FT, :], [(h_ready, G + UP)])

            for credited in (s_exp, gate_th):
                act.sem_inc(credited, CREDIT)
            act.wait_ge(lam_sum, 1)
            act.activation(lexp[:, :], lsum[:, :], ACT.Exp).then_inc(lam_exp, 1)
            act.wait_ge(x_in, 16 * KT)
            act.wait_ge(params, 1)
            act.wait_ge(cleared, 3)
            with act.Fori(0, DEPTH) as L:
                split(L, 0, 0, first=True)
                split(L, 1, 1, first=True)
                ffn(L, 0, 0, 0)
                split(L, M0, 1)
                post(L, 0)
                split(L, M0 + 1, 0)
                pre(L, 1)
                rms(L, 1)
                with act.Fori(0, PAIRS) as i:
                    A = L * PAIRS + i
                    s = M0 + i * ATT

                    def qk(hh):
                        act.wait_ge(z_ready, A * 3 + 2)
                        if hh:
                            act.wait_ge(s_ready, A * 8 + 4)
                        act.activation(qh[:, :], zq[:, hh, :], ACT.Copy)
                        act.activation(kh[0:HD, 0, :], zk[0:HD, hh, :], ACT.Copy)
                        act.activation(kh[HD:P, 1, :], zk[HD:P, hh, :], ACT.Copy).then_inc(q_hi, 1)

                    def softmax(j):
                        act.wait_ge(s_max, A * 8 + j + 1)
                        for c in range(2):
                            act.activation(pm[:, c, :], PS[:, SC + c, :], ACT.Exp, bias=nmx[:, j % 2, c:c + 1], scale=SCALE,
                                           accum_out=psums[:, j % 2, c:c + 1]).then_inc(s_exp, 1)
                        act.wait_ge(c_ready, A * 8 + j + 1)
                        act.activation(pm[:, 1, :], pm[:, 1, :], ACT.Copy, scale=c1[:, 1:2]).then_inc(p_scaled, 1)

                    def a_evac(j):
                        act.wait_ge(a_tr, A * 8 + j + 1)
                        if j % 4 == 0:
                            act.wait_ge(pv, A * 2 + j // 4 + CREDIT)
                        act.activation(aT[:, 0, :, (j % 4) * P:(j % 4 + 1) * P],
                                       PS[:, TR, :].rearrange("p (k q) -> p k q", q=P), ACT.Copy).then_inc(a_hi, 1)

                    def v_evac(hh):
                        act.wait_ge(v_tr, A * 2 + hh + 1)
                        act.activation(vh[:, :, :], PS[:, TR, :].rearrange("p (k q) -> p k q", q=P), ACT.Copy).then_inc(v_hi, 1)

                    def o_evac(hh):
                        act.wait_ge(pv, A * 2 + hh + 1 + CREDIT)
                        act.activation(sq[:, hh, :], PS[:, OB, :], ACT.Square)
                        act.activation(hid[:, ds(i * 2 + 8 + hh, 1), :], PS[:, OB, :].unsqueeze(1), ACT.Copy).then_inc(o_sq, 1)

                    split(L, s + 2, 1)
                    split(L, s + 3, 0)
                    split(L, s + 4, 1)
                    qk(0)
                    softmax(0)
                    v_evac(0)
                    softmax(1)
                    a_evac(0)
                    softmax(2)
                    a_evac(1)
                    softmax(3)
                    split(L, s + 5, 0)
                    qk(1)
                    a_evac(2)
                    softmax(4)
                    a_evac(3)
                    softmax(5)
                    o_evac(0)
                    a_evac(4)
                    softmax(6)
                    split(L, s + 6, 1)
                    v_evac(1)
                    a_evac(5)
                    softmax(7)
                    a_evac(6)
                    a_evac(7)
                    o_evac(1)
                    split(L, s + 7, 0)

                def gate(n, g, t, dst):
                    act.wait_ge(gate_z, L * 8 + 4 * g + t + 1)
                    for j in range(2):
                        ins = act.activation(dst[:, j, :], gatez[:, j, :], ACT.Tanh, scale=0.5,
                                             bias=bg[:, ds(L, 1), g, 2 * t + j])
                    ins.then_inc(gate_th, 1)

                for t in range(4):
                    if t < 2:
                        split(L, GC0 + t + 2, (GC0 + t) % 2)
                    else:
                        split(L, GC0 + t + 2, (GC0 + t) % 2, hid[:, 2 * t - 4:2 * t - 2, :], [(conv_done, L * PAIRS + t - 1)])
                    gate(GC0, 0, t, yw[:, 2 * t:2 * t + 2, :])
                for t in range(4):
                    if t < 2:
                        split(L, CO0 + t + 2, (CO0 + t) % 2, hid[:, 2 * t + 4:2 * t + 6, :], [(conv_done, L * PAIRS + t + 3)])
                    else:
                        split(L, CO0 + t + 2, (CO0 + t) % 2, hid[:, 2 * t + 4:2 * t + 6, :], [(o_done, L * HEADS + 2 * t - 2 + CREDIT)])
                for t in range(2):
                    split(L, AO0 + t + 2, (AO0 + t) % 2, hid[:, 2 * t + 12:2 * t + 14, :], [(o_done, L * HEADS + 2 * t + 6 + CREDIT)])
                split(L, AO0 + 4, AO0 % 2)
                for m in range(KT):
                    act.wait_ge(y_ready, L * (5 * KT) + 2 * KT + m + 1)
                    act.activation(hid[:, 8 + m, :], PS[:, m, :], ACT.Copy, scale=0.5).then_inc(ao_read, 1)
                split(L, AO0 + 5, (AO0 + 1) % 2)
                for t in range(4):
                    if t < 2:
                        split(L, GA0 + t + 2, (GA0 + t) % 2)
                    else:
                        split(L, GA0 + t + 2, (GA0 + t) % 2, hid[:, 2 * t - 4:2 * t - 2, :], [(m_ready, L * 4 + t - 1)])
                    gate(GA0, 1, t, gateth)
                for t in range(3):
                    if t < 2:
                        split(L, WO0 + t + 2, (WO0 + t) % 2, hid[:, 2 * t + 4:2 * t + 6, :], [(m_ready, L * 4 + t + 3)])
                    else:
                        split(L, F20, F20 % 2)
                post(L, 1)
                split(L, F20 + 1, (F20 + 1) % 2)
                ffn(L, 1, F20, 2)
                post(L, 2)

        @block.tensor
        def _(pe):
            pe.wait_ge(consts_in, 16 * 9)
            pe.wait_ge(cleared, 3)
            pe.sem_inc(pv, CREDIT)

            def product(bank, slot, off, xhi, xlo, start, stop):
                hi, lo = wh[:, slot, off:off + P], wl[:, slot, off:off + P]
                pe.matmul(PS[:, bank, :], hi, xhi, start=start, stop=False)
                pe.matmul(PS[:, bank, :], hi, xlo, start=False, stop=False)
                return pe.matmul(PS[:, bank, :], lo, xhi, start=False, stop=stop)

            def wide_ops(L, s, slot, ordinal, banks, norm=None):
                def step(k, j):
                    def run():
                        if k == 0 and j == 0:
                            pe.wait_ge(w_lo, L * STAGES + s + (RAW_CREDIT + 1))
                            pe.wait_ge(wide_read, L * WIDE + ordinal + (READ_CREDIT - 1))
                        if norm is not None and j == 0:
                            pe.wait_ge(xw_ready, L * (3 * KT) + norm * KT + k + 1)
                        mm = product(banks + j, slot, k * 256 + j * P, xh[:, k, :], xl[:, k, :], k == 0, k == KT - 1)
                        if k == KT - 1 and j == 1:
                            mm.then_inc(w_used, 1)
                    return run
                return [step(k, j) for k in range(KT) for j in range(2)]

            def wide_stage(*a, **kw):
                for op in wide_ops(*a, **kw):
                    op()

            def norm_stat(L, n):
                pe.wait_ge(acc_done, L * 36 + n * 6 + 6)
                pe.wait_ge(sq_ready, L * (6 * KT) + n * KT + KT)
                for t in range(TT):
                    pe.matmul(PS[:, 4, t:t + 1], acc[:, t * P:(t + 1) * P], ones[:, 0:1], start=True, stop=False)
                    mm = pe.matmul(PS[:, 4, t:t + 1], sq[:, 1, t * P:(t + 1) * P], ones[:, 0:1], start=False, stop=True)
                mm.then_inc(stat, 1)

            def norm_wide(L, n):
                pe.wait_ge(diag_ready, L * 6 + n + 1)
                pe.matmul(PS[:, 5, :], ones[:, :], diag[:, :, :], start=True, stop=True).then_inc(wide, 1)

            def deep_stage(L, s, slot, first, last, bank_free=None, y=None):
                pe.wait_ge(w_lo, L * STAGES + s + (RAW_CREDIT + 1))
                for m in (list(range(KT)) if last or bank_free is None else [4, 5, 6, 7, 0, 1, 2, 3]):
                    if bank_free is not None:
                        bank_free(m)
                    for kk in range(2):
                        mm = product(m, slot, kk * D + m * P, jit[:, slot, 0, kk, :], jit[:, slot, 1, kk, :],
                                     first and kk == 0, last and kk == 1)
                    if last:
                        mm.then_inc(y_ready, 1)
                if last:
                    pe.drain()
                    pe.sem_inc(w_used, 1)
                else:
                    mm.then_inc(w_used, 1)

            def ffn(L, s0, ordinal, n):
                a = s0 % 2
                wide_stage(L, s0, a, ordinal, 0, norm=n)
                norm_stat(L, 2 * n)
                wide_stage(L, s0 + 1, 1 - a, ordinal + 1, 2)
                norm_wide(L, 2 * n)
                with pe.Fori(1, UP) as i:
                    wide_stage(L, s0 + i * 2, a, ordinal + i * 2, 0)
                    wide_stage(L, s0 + i * 2 + 1, 1 - a, ordinal + i * 2 + 1, 2)
                s1 = s0 + 2 * UP

                def free(m):
                    if m == 0:
                        pe.wait_ge(wide_read, L * WIDE + ordinal + 2 * UP + READ_CREDIT)
                deep_stage(L, s1, a, True, False, free)
                with pe.Fori(0, (UP - 3) // 2 + 0) as i:
                    deep_stage(L, s1 + i * 2 + 1, 1 - a, False, False)
                    deep_stage(L, s1 + i * 2 + 2, a, False, False)
                deep_stage(L, s1 + UP - 2, 1 - a, False, False)
                deep_stage(L, s1 + UP - 1, a, False, True)
                norm_stat(L, 2 * n + 1)
                norm_wide(L, 2 * n + 1)

            with pe.Fori(0, DEPTH) as L:
                ffn(L, 0, 0, 0)
                norm_stat(L, 2)
                norm_wide(L, 2)
                o0 = 2 * UP
                with pe.Fori(0, PAIRS) as i:
                    A = L * PAIRS + i
                    ops = [wide_ops(L, M0 + i * ATT + n, (M0 + n) % 2, o0 + i * ATT + n, 2 * (n % 2), norm=1 if n == 0 else None) for n in range(ATT)]
                    for n in range(3):
                        for op in ops[n]:
                            op()
                    flow = ops[3] + ops[4] + ops[5]

                    def stage_work(n):
                        for _ in range(n):
                            flow.pop(0)()

                    def scores(j):
                        hh, qt = j // 4, j % 4
                        if qt == 0:
                            pe.wait_ge(qk_lo, A * 2 + hh + 1)
                        pe.wait_ge(s_exp, A * 16 + 2 * j + CREDIT)
                        q = slice(qt * P, (qt + 1) * P)
                        for c in range(2):
                            pe.matmul(PS[:, SC + c, :], qh[:, q], kh[:, c, :], start=True, stop=False)
                            pe.matmul(PS[:, SC + c, :], qh[:, q], kl[:, c, :], start=False, stop=False)
                            mm = pe.matmul(PS[:, SC + c, :], ql[:, q], kh[:, c, :], start=False, stop=True)
                        mm.then_inc(s_ready, 1)

                    def a_transpose(j):
                        pe.wait_ge(a_ready, A * 8 + j + 1)
                        pe.wait_ge(a_lo, A * 8 + j + CREDIT)
                        pe.wait_ge(v_lo, A * 2 + (1 if j < 5 else 2))
                        for kt in range(TT):
                            mm = pe.transpose(PS[:, TR, kt * P:(kt + 1) * P], att[:, j % 2, kt * P:(kt + 1) * P], ident[:, :])
                        mm.then_inc(a_tr, 1)

                    def v_transpose(hh):
                        pe.wait_ge(z_ready, A * 3 + 3)
                        pe.wait_ge(a_lo, A * 8 + (5 if hh else 0) + CREDIT)
                        for kt in range(TT):
                            mm = pe.transpose(PS[:, TR, kt * P:(kt + 1) * P], zv[:, hh, kt * P:(kt + 1) * P], ident[:, :])
                        mm.then_inc(v_tr, 1)

                    def values(hh):
                        pe.wait_ge(a_lo, A * 8 + 4 * hh + 4 + CREDIT)
                        pe.wait_ge(v_lo, A * 2 + hh + 1)
                        pe.wait_ge(o_done, A * 2 + hh + CREDIT)
                        for kt in range(TT):
                            pe.matmul(PS[:, OB, :], vh[:, kt, :], aT[:, 0, kt, :], start=(kt == 0), stop=False)
                            pe.matmul(PS[:, OB, :], vh[:, kt, :], aT[:, 1, kt, :], start=False, stop=False)
                            mm = pe.matmul(PS[:, OB, :], vl[:, kt, :], aT[:, 0, kt, :], start=False, stop=(kt == TT - 1))
                        mm.then_inc(pv, 1)

                    def out_stat(hh):
                        pe.wait_ge(o_sq, A * 2 + hh + 1)
                        for t in range(TT):
                            mm = pe.matmul(PS[:, OB, t:t + 1], sq[:, hh, t * P:(t + 1) * P], ones[:, 0:1], start=True, stop=True)
                        mm.then_inc(o_stat, 1)

                    def out_wide(hh):
                        pe.wait_ge(o_diag, A * 2 + hh + 1)
                        pe.matmul(PS[:, OB, :], ones[:, :], diag[:, :, :], start=True, stop=True).then_inc(o_wide, 1)

                    scores(0)
                    stage_work(5)
                    v_transpose(0)
                    scores(1)
                    stage_work(5)
                    a_transpose(0)
                    scores(2)
                    stage_work(5)
                    a_transpose(1)
                    scores(3)
                    stage_work(5)
                    a_transpose(2)
                    scores(4)
                    stage_work(5)
                    a_transpose(3)
                    scores(5)
                    stage_work(5)
                    values(0)
                    a_transpose(4)
                    scores(6)
                    stage_work(3)
                    v_transpose(1)
                    stage_work(2)
                    out_stat(0)
                    a_transpose(5)
                    scores(7)
                    stage_work(4)
                    out_wide(0)
                    a_transpose(6)
                    stage_work(2)
                    a_transpose(7)
                    stage_work(2)
                    values(1)
                    stage_work(2)
                    out_stat(1)
                    stage_work(3)
                    out_wide(1)

                o1 = o0 + ATT * PAIRS
                for t in range(4):
                    wide_stage(L, GC0 + t, (GC0 + t) % 2, o1 + t, 2 * (t % 2))
                for t in range(4):
                    def gates_read(m):
                        if m == 0:
                            pe.wait_ge(wide_read, L * WIDE + o1 + 4 + READ_CREDIT)
                        if m == 4:
                            pe.wait_ge(o_done, L * HEADS + HEADS + CREDIT)
                    deep_stage(L, CO0 + t, (CO0 + t) % 2, t == 0, t == 3, gates_read if t == 0 else None)
                for t in range(4):
                    def conv_read(m):
                        pe.wait_ge(co_read, L * KT + (m + 1 if m < 4 else 8))
                    deep_stage(L, AO0 + t, (AO0 + t) % 2, t == 0, t == 3, conv_read if t == 0 else None)
                pe.wait_ge(ao_read, L * KT + KT)
                for t in range(4):
                    wide_stage(L, GA0 + t, (GA0 + t) % 2, o1 + 4 + t, 2 * (t % 2))
                for t in range(4):
                    def gates_read2(m):
                        if m == 0:
                            pe.wait_ge(wide_read, L * WIDE + o1 + 8 + READ_CREDIT)
                    deep_stage(L, WO0 + t, (WO0 + t) % 2, t == 0, t == 3, gates_read2 if t == 0 else None)
                norm_stat(L, 3)
                norm_wide(L, 3)
                ffn(L, F20, o1 + 8, 2)

        @block.vector
        def _(dve):
            for _ in range(RAW_CREDIT):
                dve.memset(rv[:, :], 0.0).then_inc(w_lo, 1)
                dve.drain()
            for credited in (a_lo, o_done, x_ready):
                dve.sem_inc(credited, CREDIT)
            for _ in range(READ_CREDIT):
                dve.drain()
                dve.memset(rv[:, :], 0.0).then_inc(wide_read, 1)
            dve.wait_ge(consts_in, 16 * 9)
            for n in (1, 5):
                dve.tensor_scalar(nw[:, :, n, :], nw[:, :, n, :], 0.5, None, ALU.mult)
            dve.tensor_scalar(bg[:, :, :, :], bg[:, :, :, :], 0.5, None, ALU.mult)
            dve.tensor_tensor(sub[:, :], sub[:, :], lamc[:, 1, :], ALU.mult)
            lv = lamv.rearrange("p (l a b d) -> p (l a) b d", l=DEPTH, a=2, b=2)
            prod = hid[:, 1, 0:DEPTH * 2 * HD].rearrange("p (l d) -> p l d", d=HD)
            dve.tensor_tensor(prod, lv[:, :, 0, :], lv[:, :, 1, :], ALU.mult)
            dve.drain()
            dve.tensor_reduce(lsum[:, :], prod, AX.X, ALU.add).then_inc(lam_sum, 1)
            dve.wait_ge(lam_exp, 1)
            le = lexp[:, :].rearrange("p (l a) -> p l a", a=2)
            dve.tensor_tensor(nlam[:, :], le[:, :, 1], le[:, :, 0], ALU.subtract)
            dve.drain()
            dve.tensor_tensor(nlam[:, :], nlam[:, :], lamc[:, 0, :], ALU.subtract).then_inc(params, 1)
            dve.drain()

            def rsqrt(bank_cols, count, done):
                dve.tensor_scalar(rv[:, :], bank_cols, 1.0 / count, EPS, ALU.mult, ALU.add)
                dve.drain()
                dve.tensor_scalar(rt[:, :].bitcast(i32), rv[:, :].bitcast(i32), 1, None, ALU.logical_shift_right)
                dve.drain()
                dve.tensor_scalar(ry[:, :].bitcast(i32), rt[:, :].bitcast(i32), -1.0, float(0x5F3759DF), ALU.mult, ALU.add)
                for _ in range(3):
                    dve.drain()
                    dve.tensor_tensor(rt[:, :], ry[:, :], ry[:, :], ALU.mult)
                    dve.drain()
                    dve.scalar_tensor_tensor(out=rt[:, :], in0=rt[:, :], scalar=-0.5, in1=rv[:, :], op0=ALU.mult, op1=ALU.mult)
                    dve.drain()
                    dve.scalar_tensor_tensor(out=ry[:, :], in0=rt[:, :], scalar=1.5, in1=ry[:, :], op0=ALU.add, op1=ALU.mult)
                dve.drain()
                dve.tensor_tensor(diag[:, :, :], ident[:, :].unsqueeze(1).to_broadcast([P, TT, P]),
                                  ry[:, :].unsqueeze(2).to_broadcast([P, TT, P]), ALU.mult).then_inc(done, 1)
                dve.drain()

            def split(L, s, slot, src=None):
                dve.wait_ge(w_hi, L * STAGES + s + 1)
                if src is not None:
                    dve.tensor_tensor(jit[:, slot, 1, :, :], src, jit[:, slot, 0, :, :].bitcast(f32), ALU.subtract)
                dve.tensor_tensor(wl[:, slot, :], raw[:, slot, :], wh[:, slot, :].bitcast(f32), ALU.subtract).then_inc(w_lo, 1)

            def pre(L, n):
                for k in range(KT):
                    dve.wait_ge(x_hi, L * (3 * KT) + n * KT + k + 1)
                    dve.scalar_tensor_tensor(out=xl[:, k, :], in0=x[:, k, :], scalar=nw[:, ds(L, 1), 2 * n, k],
                                             in1=xh[:, k, :].bitcast(f32), op0=ALU.mult, op1=ALU.subtract).then_inc(xw_ready, 1)
                dve.wait_ge(stat, L * 6 + 2 * n + 1)
                rsqrt(PS[:, 4, 0:TT], D, diag_ready)

            def post(L, n):
                dve.wait_ge(stat, L * 6 + 2 * n + 2)
                rsqrt(PS[:, 4, 0:TT], D, diag_ready)
                dve.wait_ge(wide, L * 6 + 2 * n + 2)
                dve.wait_ge(y_scaled, L * (3 * KT) + n * KT + KT)
                for k in range(KT):
                    dve.tensor_tensor(yw[:, k, :], PS[:, 5, :], yw[:, k, :], ALU.mult)
                    dve.drain()
                    dve.tensor_tensor(x[:, k, :], x[:, k, :], yw[:, k, :], ALU.add).then_inc(x_ready, 1)

            def rows(t):
                return t.unsqueeze(1).to_broadcast([P, 2, T])

            def scaled(dst, bank, done):
                dve.tensor_tensor(dst, PS[:, bank:bank + 2, :], rows(rpre[:, :]), ALU.mult).then_inc(done, 1)

            def used(L, s):
                dve.wait_ge(w_used, L * STAGES + s + 1)

            def ffn(L, w, s0, n):
                a = s0 % 2
                G = (L * 2 + w) * UP
                pre(L, n)

                def step(i, s, last):
                    split(L, s + 2, a, hid[:, 0:2, :] if last else None)
                    used(L, s)
                    dve.wait_ge(r_ready, L * 3 + n + 1)
                    scaled(gz, 0, wide_read)
                    dve.drain()
                    dve.sem_inc(gz_ready, 1)
                    split(L, s + 3, 1 - a, hid[:, 2:4, :] if last else None)
                    used(L, s + 1)
                    scaled(uz, 2, wide_read)
                    dve.wait_ge(th_ready, G + i + 1)
                    dve.scalar_tensor_tensor(out=gz, in0=th, scalar=1.0, in1=gz, op0=ALU.add, op1=ALU.mult)
                    dve.drain()
                    dve.scalar_tensor_tensor(out=hid[:, ds(i * 2, 2), :], in0=gz, scalar=0.5, in1=uz,
                                             op0=ALU.mult, op1=ALU.mult).then_inc(h_ready, 1)
                    dve.drain()

                with dve.Fori(0, UP - 1) as i:
                    step(i, s0 + i * 2, False)
                step(UP - 1, s0 + 2 * (UP - 1), True)
                s1 = s0 + 2 * UP
                with dve.Fori(0, (UP - 3) // 2) as i:
                    split(L, s1 + i * 2 + 2, a, hid[:, ds(i * 4 + 4, 2), :])
                    split(L, s1 + i * 2 + 3, 1 - a, hid[:, ds(i * 4 + 6, 2), :])
                split(L, s1 + UP - 1, a, hid[:, FT - 2:FT, :])

            with dve.Fori(0, DEPTH) as L:
                split(L, 0, 0)
                split(L, 1, 1)
                ffn(L, 0, 0, 0)
                split(L, M0, 1)
                post(L, 0)
                split(L, M0 + 1, 0)
                pre(L, 1)
                with dve.Fori(0, PAIRS) as i:
                    A = L * PAIRS + i
                    s = M0 + i * ATT

                    def rope(z, bank):
                        scaled(z, bank, wide_read)
                        dve.drain()
                        for hh in range(2):
                            dve.stream_shuffle(shuf, z[:, hh, :], list(range(8, 16)) + list(range(8)) + list(range(16, 32)))
                            dve.drain()
                            dve.tensor_tensor(shuf, shuf, sinT[:, :], ALU.mult)
                            dve.tensor_tensor(z[:, hh, :], z[:, hh, :], cosT[:, :], ALU.mult)
                            dve.drain()
                            ins = dve.tensor_tensor(z[:, hh, :], z[:, hh, :], shuf, ALU.add)
                            if hh == 0:
                                dve.drain()
                        ins.then_inc(z_ready, 1)

                    def qk(hh):
                        dve.wait_ge(q_hi, A * 2 + hh + 1)
                        dve.tensor_tensor(ql[:, :], zq[:, hh, :], qh[:, :].bitcast(f32), ALU.subtract)
                        dve.tensor_tensor(kl[0:HD, 0, :], zk[0:HD, hh, :], kh[0:HD, 0, :].bitcast(f32), ALU.subtract)
                        dve.tensor_tensor(kl[HD:P, 1, :], zk[HD:P, hh, :], kh[HD:P, 1, :].bitcast(f32), ALU.subtract) \
                           .then_inc(qk_lo, 1)

                    def row_max(j):
                        dve.wait_ge(s_ready, A * 8 + j + 1)
                        dve.tensor_reduce(mx[:, :], PS[:, SC:SC + 2, :], AX.X, ALU.max)
                        dve.drain()
                        dve.tensor_scalar(nmx[:, j % 2, :], mx[:, :], -SCALE, None, ALU.mult).then_inc(s_max, 1)

                    def combine(j):
                        dve.wait_ge(s_exp, A * 16 + 2 * j + 2 + CREDIT)
                        dve.reciprocal(rsum[:, :], psums[:, j % 2, :])
                        dve.drain()
                        dve.tensor_scalar(c1[:, 1:2], rsum[:, 1:2], nlam[:, ds(L, 1)], None, ALU.mult).then_inc(c_ready, 1)
                        dve.wait_ge(p_scaled, A * 8 + j + 1)
                        if j >= 2:
                            dve.wait_ge(a_tr, A * 8 + j - 1)
                        dve.scalar_tensor_tensor(out=att[:, j % 2, :], in0=pm[:, 0, :], scalar=rsum[:, 0:1], in1=pm[:, 1, :],
                                                 op0=ALU.mult, op1=ALU.add).then_inc(a_ready, 1)

                    def a_evac(j):
                        dve.wait_ge(a_hi, A * 8 + j + 1)
                        sl = slice((j % 4) * P, (j % 4 + 1) * P)
                        dve.tensor_tensor(aT[:, 1, :, sl], PS[:, TR, :].rearrange("p (k q) -> p k q", q=P),
                                          aT[:, 0, :, sl].bitcast(f32), ALU.subtract).then_inc(a_lo, 1)

                    def v_evac(hh):
                        dve.wait_ge(v_hi, A * 2 + hh + 1)
                        dve.tensor_tensor(vl[:, :, :], PS[:, TR, :].rearrange("p (k q) -> p k q", q=P),
                                          vh[:, :, :].bitcast(f32), ALU.subtract).then_inc(v_lo, 1)

                    def out_norm(hh):
                        dve.wait_ge(o_stat, A * 2 + hh + 1)
                        rsqrt(PS[:, OB, 0:TT], P, o_diag)

                    def out_scale(hh):
                        dve.wait_ge(o_wide, A * 2 + hh + 1)
                        o = hid[:, ds(i * 2 + 8 + hh, 1), :]
                        dve.scalar_tensor_tensor(out=o, in0=o, scalar=sub[:, ds(L, 1)], in1=PS[:, OB, :].unsqueeze(1),
                                                 op0=ALU.mult, op1=ALU.mult).then_inc(o_done, 1)

                    def conv(hh):
                        yc = hid[:, ds(i * 2 + hh, 1), :].rearrange("p a t -> p (a t)")
                        w3 = [cw[:, ds(L, 1), n, ds(i * 2 + hh, 1)] for n in range(3)]
                        ins = dve.tensor_tensor(cu, PS[:, 2 + hh, :], rpre[:, :], ALU.mult)
                        if hh:
                            ins.then_inc(wide_read, 1)
                        dve.drain()
                        dve.tensor_tensor(cu, cu, yc, ALU.mult)
                        dve.drain()
                        dve.tensor_scalar(yc, cu, w3[1], None, ALU.mult)
                        dve.drain()
                        dve.scalar_tensor_tensor(out=yc[:, 1:T], in0=cu[:, 0:T - 1], scalar=w3[0], in1=yc[:, 1:T],
                                                 op0=ALU.mult, op1=ALU.add)
                        dve.drain()
                        dve.scalar_tensor_tensor(out=yc[:, 0:T - 1], in0=cu[:, 1:T], scalar=w3[2], in1=yc[:, 0:T - 1],
                                                 op0=ALU.mult, op1=ALU.add)
                        dve.drain()
                        return dve.tensor_tensor(yc, yc, convb[:, hh, :], ALU.mult)

                    dve.wait_ge(r_ready, L * 3 + 2)
                    used(L, s)
                    rope(zq, 0)
                    split(L, s + 2, 1)
                    used(L, s + 1)
                    rope(zk, 2)
                    split(L, s + 3, 0)
                    used(L, s + 2)
                    scaled(zv, 0, wide_read)
                    dve.drain()
                    dve.sem_inc(z_ready, 1)
                    split(L, s + 4, 1)
                    qk(0)
                    row_max(0)
                    combine(0)
                    v_evac(0)
                    row_max(1)
                    combine(1)
                    a_evac(0)
                    row_max(2)
                    combine(2)
                    a_evac(1)
                    row_max(3)
                    combine(3)
                    used(L, s + 3)
                    scaled(convb, 2, wide_read)
                    split(L, s + 5, 0)
                    qk(1)
                    a_evac(2)
                    row_max(4)
                    combine(4)
                    a_evac(3)
                    row_max(5)
                    combine(5)
                    a_evac(4)
                    row_max(6)
                    combine(6)
                    used(L, s + 4)
                    scaled(hid[:, ds(i * 2, 2), :], 0, wide_read)
                    split(L, s + 6, 1)
                    v_evac(1)
                    out_norm(0)
                    a_evac(5)
                    row_max(7)
                    combine(7)
                    out_scale(0)
                    a_evac(6)
                    a_evac(7)
                    out_norm(1)
                    used(L, s + 5)
                    conv(0)
                    dve.drain()
                    conv(1).then_inc(conv_done, 1)
                    out_scale(1)
                    split(L, s + 7, 0)
                    dve.drain()

                for t in range(4):
                    if t < 2:
                        split(L, GC0 + t + 2, (GC0 + t) % 2)
                    else:
                        split(L, GC0 + t + 2, (GC0 + t) % 2, hid[:, 2 * t - 4:2 * t - 2, :])
                    used(L, GC0 + t)
                    dve.wait_ge(gate_th, L * 8 + t + CREDIT)
                    scaled(gatez, 2 * (t % 2), wide_read)
                    dve.drain()
                    dve.sem_inc(gate_z, 1)
                for t in range(3):
                    split(L, CO0 + t + 2, (CO0 + t) % 2, hid[:, 2 * t + 4:2 * t + 6, :])
                dve.wait_ge(gate_th, L * 8 + 4 + CREDIT)
                for m in range(KT):
                    dve.wait_ge(y_ready, L * (5 * KT) + KT + m + 1)
                    dve.scalar_tensor_tensor(out=hid[:, m, :], in0=yw[:, m, :], scalar=1.0, in1=PS[:, m, :],
                                             op0=ALU.add, op1=ALU.mult).then_inc(co_read, 1)
                split(L, CO0 + 5, (CO0 + 3) % 2, hid[:, 10:12, :])
                for t in range(4):
                    if t < 2:
                        split(L, AO0 + t + 2, (AO0 + t) % 2, hid[:, 2 * t + 12:2 * t + 14, :])
                    else:
                        split(L, AO0 + t + 2, (AO0 + t) % 2)
                dve.wait_ge(ao_read, L * KT + KT)
                for t in range(4):
                    if t < 2:
                        split(L, GA0 + t + 2, (GA0 + t) % 2)
                    else:
                        split(L, GA0 + t + 2, (GA0 + t) % 2, hid[:, 2 * t - 4:2 * t - 2, :])
                    used(L, GA0 + t)
                    scaled(gatez, 2 * (t % 2), wide_read)
                    dve.drain()
                    dve.sem_inc(gate_z, 1)
                    dve.wait_ge(gate_th, L * 8 + 5 + t + CREDIT)
                    dve.scalar_tensor_tensor(out=gateth, in0=gateth, scalar=1.0, in1=hid[:, 8 + 2 * t:10 + 2 * t, :],
                                             op0=ALU.add, op1=ALU.mult)
                    dve.drain()
                    dve.scalar_tensor_tensor(out=hid[:, 2 * t:2 * t + 2, :], in0=hid[:, 2 * t:2 * t + 2, :], scalar=0.5,
                                             in1=gateth, op0=ALU.mult, op1=ALU.add).then_inc(m_ready, 1)
                    dve.drain()
                for t in range(3):
                    if t < 2:
                        split(L, WO0 + t + 2, (WO0 + t) % 2, hid[:, 2 * t + 4:2 * t + 6, :])
                    else:
                        split(L, F20, F20 % 2)
                post(L, 1)
                split(L, F20 + 1, (F20 + 1) % 2)
                ffn(L, 1, F20, 2)
                post(L, 2)


def rope_tables():
    rot = HD // 4
    half = rot // 2
    inv = (np.float32(500000.0) ** (-np.arange(0, rot, 2, dtype=np.float32) / np.float32(rot))).astype(np.float32)
    ang = np.arange(T, dtype=np.float32)[None, :] * inv[:, None]
    cos, sin = np.cos(ang).astype(np.float32), np.sin(ang).astype(np.float32)
    C, S = np.ones((P, T), np.float32), np.zeros((P, T), np.float32)
    for base in (0, HD):
        C[base:base + half], C[base + half:base + rot] = cos, cos
        S[base:base + half], S[base + half:base + rot] = -sin, sin
    return C, S


def kernel(**inputs):
    import concourse.bacc as _bacc
    from concourse.bass_utils import run_bass_kernel_spmd as _run

    a = {k: np.asarray(v) for k, v in inputs.items()}
    C, S = rope_tables()
    init = [0.8 - 0.6 * math.exp(-0.3 * l) for l in range(DEPTH)]
    lam_const = np.broadcast_to(np.array(init + [1.0 - v for v in init], np.float32), (P, 2 * DEPTH))

    def columns(v):
        return v.reshape(-1, P).T

    arrays = {
        "xT": a["x"][0].T, "w_in": a["w_in"], "w_conv_out": a["w_conv_out"], "w_attn_out": a["w_attn_out"],
        "w_o": a["w_o"], "ffn1_w13": a["ffn1_w13"], "ffn1_w2": a["ffn1_w2"], "ffn2_w13": a["ffn2_w13"],
        "ffn2_w2": a["ffn2_w2"], "norm_wT": columns(a["norm_w"]), "b_gateT": columns(a["b_gate"]),
        "conv_wT": columns(a["conv_w"]), "sublnT": columns(a["subln_w"]), "lam_vec": a["lam_vec"],
        "ropeC": C, "ropeS": S, "ident_in": np.eye(P, dtype=np.float32), "lam_const": lam_const,
    }
    arrays = {f"in_{k}": np.ascontiguousarray(v) for k, v in arrays.items()}
    nc = _bacc.Bacc("TRN2", target_bir_lowering=False, num_devices=1)
    args = [nc.dram_tensor(k, v.shape, mybir.dt.from_np(v.dtype), kind="ExternalInput").ap() for k, v in arrays.items()]
    out = nc.dram_tensor("out_0", (D, T), mybir.dt.float32, kind="ExternalOutput").ap()
    encoder_kernel(nc, *args, out)
    r = _run(nc, [arrays], core_ids=[0])
    return np.ascontiguousarray(r.results[0]["out_0"].T)[None]
```

```python
import math

import numpy as np
import concourse.bass as bass
from concourse import mybir
from contextlib import ExitStack

DEPTH = 2
D = 1024
T = 512
DFF = 2816
HEADS = 8
P = 128
KT = D // P
FT = DFF // P
UP = FT // 2
TT = T // P
HD = 64
EPS = 1e-6
SCALE = HD ** -0.5
STAGE = 2048

FFN = 2 * UP + UP
PAIRS = HEADS // 2
ATT = 6
MIX = ATT * PAIRS + 4 * 4 + 4
STAGES = 2 * FFN + MIX
M0 = FFN
GC0 = M0 + ATT * PAIRS
CO0 = GC0 + 4
AO0 = CO0 + 4
GA0 = AO0 + 4
WO0 = GA0 + 4
F20 = M0 + MIX
WIDE = 2 * 2 * UP + ATT * PAIRS + 8
RAW_CREDIT = 2
READ_CREDIT = 2
CREDIT = 1


def encoder_kernel(nc, xT, w_in, w_conv_out, w_attn_out, w_o, ffn1_w13, ffn1_w2, ffn2_w13, ffn2_w2,
                   norm_wT, b_gateT, conv_wT, sublnT, lam_vec, ropeC, ropeS, ident_in, lam_const, out):
    f32, f32r, i32 = mybir.dt.float32, mybir.dt.float32r, mybir.dt.int32
    ALU, ACT, AX = mybir.AluOpType, mybir.ActivationFunctionType, mybir.AxisListType
    ds = bass.ds

    with ExitStack() as ctx:
        def sb(name, shape, dt=f32):
            return ctx.enter_context(nc.sbuf_tensor(name, shape, dt))

        def sem(name):
            return ctx.enter_context(nc.semaphore(name))

        x = sb("x", [P, KT, T])
        xh = sb("xh", [P, KT, T], f32r)
        xl = sb("xl", [P, KT, T], f32r)
        yw = sb("yw", [P, KT, T])
        hid = sb("hid", [P, FT, T])
        raw = sb("raw", [P, 2, STAGE])
        wh = sb("wh", [P, 2, STAGE], f32r)
        wl = sb("wl", [P, 2, STAGE], f32r)
        jit = sb("jit", [P, 2, 2, 2, T], f32r)
        aT = jit[:, :, :, :, :].rearrange("p a b c t -> p a (b c) t")
        qh = sb("qh", [P, T], f32r)
        ql = sb("ql", [P, T], f32r)
        kh = sb("kh", [P, 2, T], f32r)
        kl = sb("kl", [P, 2, T], f32r)
        vh = sb("vh", [P, TT, 2, P], f32r)
        vl = sb("vl", [P, TT, 2, P], f32r)
        cosT = sb("cosT", [P, T])
        sinT = sb("sinT", [P, T])
        rpre = sb("rpre", [P, T])
        acc = sb("acc", [P, T])
        sq = sb("sq", [P, 2, T])
        diag = sq[:, 0, :].rearrange("p (t c) -> p t c", c=P)
        ones = sb("ones", [P, P])
        ident = sb("ident", [P, P])
        nw = sb("nw", [P, DEPTH, 6, KT])
        bg = sb("bg", [P, DEPTH, 2, KT])
        cw = sb("cw", [P, DEPTH, 3, KT])
        sub = sb("sub", [P, DEPTH])
        lamc = sb("lamc", [P, 2, DEPTH])
        nlam = sb("nlam", [P, DEPTH])
        lsum = sb("lsum", [P, 2 * DEPTH])
        lexp = sb("lexp", [P, 2 * DEPTH])
        rv = sb("rv", [P, TT])
        rt = sb("rt", [P, TT])
        ry = sb("ry", [P, TT])
        mx = sb("mx", [P, 2])
        nmx = sb("nmx", [P, 2, 2])
        psums = sb("psums", [P, 2, 2])
        rsum = sb("rsum", [P, 2])
        rtall = sb("rtall", [P, TT])
        gz, th, uz = yw[:, 0:2, :], yw[:, 2:4, :], yw[:, 4:6, :]
        zq, zk, shuf = yw[:, 0:2, :], yw[:, 2:4, :], yw[:, 4:6, :]
        pm = yw[:, 6:8, :]
        convb = hid[:, 18:20, :]
        att = hid[:, 16:18, :]
        cu = hid[:, 20:22, :]
        gatez = hid[:, 16:18, :]
        gateth = hid[:, 18:20, :]
        lamv = hid[:, 0, 0:DEPTH * 4 * HD]
        PS = ctx.enter_context(nc.psum_tensor("PS", [P, 8, T], f32))
        SC, TR, OB = 4, 6, 7

        consts_in, x_in, y_out = sem("consts_in"), sem("x_in"), sem("y_out")
        cleared, params = sem("cleared"), sem("params")
        lam_sum, lam_exp = sem("lam_sum"), sem("lam_exp")
        w_loaded = [sem("w_loaded0"), sem("w_loaded1")]
        w_hi, w_lo, w_used = sem("w_hi"), sem("w_lo"), sem("w_used")
        x_ready, x_hi, xw_ready = sem("x_ready"), sem("x_hi"), sem("xw_ready")
        sq_ready, acc_done = sem("sq_ready"), sem("acc_done")
        stat, diag_ready, wide, r_ready = sem("stat"), sem("diag_ready"), sem("wide"), sem("r_ready")
        wide_read = sem("wide_read")
        gz_ready, th_ready, h_ready = sem("gz_ready"), sem("th_ready"), sem("h_ready")
        y_ready = sem("y_ready")
        y_scaled, co_read, ao_read = sem("y_scaled"), sem("co_read"), sem("ao_read")
        z_ready, q_hi, qk_lo = sem("z_ready"), sem("q_hi"), sem("qk_lo")
        v_hi, v_lo = sem("v_hi"), sem("v_lo")
        s_ready, s_max, s_exp = sem("s_ready"), sem("s_max"), sem("s_exp")
        a_ready = sem("a_ready")
        a_tr, a_hi, a_lo = sem("a_tr"), sem("a_hi"), sem("a_lo")
        pv, o_sq, o_stat, o_diag, o_wide, o_done = (sem("pv"), sem("o_sq"), sem("o_stat"), sem("o_diag"),
                                                    sem("o_wide"), sem("o_done"))
        conv_done = sem("conv_done")
        gate_z, gate_th, m_ready = sem("gate_z"), sem("gate_th"), sem("m_ready")
        N_CONST = 10

        block = ctx.enter_context(nc.Block())

        @block.sync
        def _(sp):
            for k in range(KT):
                sp.dma_start(x[:, k, :], xT[k * P:(k + 1) * P, :]).then_inc(x_in, 16)

            def load(L, s, slot, src):
                sp.wait_ge(w_lo, L * STAGES + s + (RAW_CREDIT - 1))
                sp.dma_start(raw[:, slot, :].rearrange("p (k c) -> p k c", c=src.shape[-1]), src) \
                    .then_inc(w_loaded[slot], 16)

            def wide_src(w, L, col):
                return w[L, :, ds(col, 256)].rearrange("(k p) c -> p k c", p=P)

            def deep_src(w, L, row):
                return w[L, ds(row, 2 * P), :].rearrange("(k p) c -> p k c", p=P)

            def ffn(L, s0, w13, w2):
                a = s0 % 2
                with sp.Fori(0, UP) as i:
                    load(L, s0 + i * 2, a, wide_src(w13, L, i * 256))
                    load(L, s0 + i * 2 + 1, 1 - a, wide_src(w13, L, i * 256 + DFF))
                s1 = s0 + 2 * UP
                with sp.Fori(0, UP // 2) as i:
                    load(L, s1 + i * 2, a, deep_src(w2, L, i * 4 * P))
                    load(L, s1 + i * 2 + 1, 1 - a, deep_src(w2, L, i * 4 * P + 2 * P))
                load(L, s1 + UP - 1, a, deep_src(w2, L, (UP - 1) * 2 * P))

            def four(L, s0, src):
                for n in range(4):
                    load(L, s0 + n, (s0 + n) % 2, src(n))

            with sp.Fori(0, DEPTH) as L:
                ffn(L, 0, ffn1_w13, ffn1_w2)
                with sp.Fori(0, PAIRS) as i:
                    for n, first in enumerate((3 * D, 4 * D, 5 * D, 0, D, 2 * D)):
                        load(L, M0 + i * ATT + n, (M0 + n) % 2, wide_src(w_in, L, i * 256 + first))
                four(L, GC0, lambda n: wide_src(w_in, L, 6 * D + n * 256))
                four(L, CO0, lambda n: deep_src(w_conv_out, L, n * 2 * P))
                four(L, AO0, lambda n: deep_src(w_attn_out, L, n * 2 * P))
                four(L, GA0, lambda n: wide_src(w_in, L, 7 * D + n * 256))
                four(L, WO0, lambda n: deep_src(w_o, L, n * 2 * P))
                ffn(L, F20, ffn2_w13, ffn2_w2)
            for k in range(KT):
                sp.wait_ge(x_ready, DEPTH * 3 * KT - KT + k + 1 + CREDIT)
                sp.dma_start(out[k * P:(k + 1) * P, :], x[:, k, :]).then_inc(y_out, 16)
            sp.wait_ge(y_out, 16 * KT)

        @block.gpsimd
        def _(pool):
            pool.memset(ones[:, :], 1.0).then_inc(cleared, 1)
            for t in (kh, kl):
                pool.memset(t[:, :, :].bitcast(f32), 0.0).then_inc(cleared, 1)

            def sums(L, n):
                for k in range(1, KT - 1):
                    pool.wait_ge(sq_ready, L * (6 * KT) + n * KT + k + 1)
                    if k > 1:
                        pool.wait_ge(acc_done, L * 36 + n * 6 + k - 1)
                    pool.tensor_tensor(acc[:, :], acc[:, :], sq[:, k % 2, :], ALU.add).then_inc(acc_done, 1)

            with pool.Fori(0, DEPTH) as L:
                with pool.Fori(0, 6) as n:
                    sums(L, n)

        @block.scalar
        def _(act):
            for dst, src in ((nw, norm_wT), (bg, b_gateT), (cw, conv_wT), (sub, sublnT), (lamc, lam_const),
                             (cosT, ropeC), (sinT, ropeS), (ident, ident_in)):
                flat = dst[:, :] if len(dst.shape) == 2 else dst[:].rearrange(
                    "p a b -> p (a b)" if len(dst.shape) == 3 else "p a b c -> p (a b c)")
                act.dma_start(flat, src[:, :]).then_inc(consts_in, 16)
            act.dma_start(lamv, lam_vec.rearrange("l a d -> (l a d)").partition_broadcast(P)).then_inc(consts_in, 16)

            def split(L, s, slot, src=None, ready=(), first=False):
                act.wait_ge(w_loaded[slot], L * (8 * STAGES) + s * 8 + (16 - 8 * slot))
                if not first:
                    act.wait_ge(w_used, L * STAGES + s - 1)
                for q, v in ready:
                    act.wait_ge(q, v)
                if src is not None:
                    act.activation(jit[:, slot, 0, :, :], src, ACT.Copy)
                act.activation(wh[:, slot, :], raw[:, slot, :], ACT.Copy).then_inc(w_hi, 1)

            def square(L, n, k, src):
                if k >= 3:
                    act.wait_ge(acc_done, L * 36 + n * 6 + k - 2)
                act.activation(acc[:, :] if k == 0 else sq[:, k % 2, :], src, ACT.Square).then_inc(sq_ready, 1)

            def pre(L, n):
                for k in range(KT):
                    act.wait_ge(x_ready, L * (3 * KT) + ((n - 1) * KT + k + 1 if n else 0) + CREDIT)
                    act.activation(xh[:, k, :], x[:, k, :], ACT.Copy, scale=nw[:, ds(L, 1), 2 * n, k]).then_inc(x_hi, 1)
                    square(L, 2 * n, k, x[:, k, :])

            def rms(L, n):
                act.wait_ge(wide, L * 6 + 2 * n + 1)
                act.activation(rpre[:, :], PS[:, 5, :], ACT.Copy).then_inc(r_ready, 1)

            def post(L, n):
                y0 = (0, 3 * KT, 4 * KT)[n]
                for m in range(KT):
                    act.wait_ge(y_ready, L * (5 * KT) + y0 + m + 1)
                    square(L, 2 * n + 1, m, PS[:, m, :])
                    act.activation(yw[:, m, :], PS[:, m, :], ACT.Copy, scale=nw[:, ds(L, 1), 2 * n + 1, m]) \
                       .then_inc(y_scaled, 1)

            def ffn(L, w, s0, n):
                a = s0 % 2
                G = (L * 2 + w) * UP
                pre(L, n)

                def step(i, s, last, first=False):
                    def up_src(ii):
                        return hid[:, ds(ii * 2, 2), :]
                    split(L, s + 2, a, None if not last else up_src(0), [(h_ready, G + 1)] if last else ())
                    if first:
                        rms(L, n)
                    act.wait_ge(gz_ready, G + i + 1)
                    act.activation(th, gz, ACT.Tanh, scale=0.5).then_inc(th_ready, 1)
                    split(L, s + 3, 1 - a, None if not last else up_src(1), [(h_ready, G + 2)] if last else ())

                step(0, s0, False, first=True)
                with act.Fori(1, UP - 1) as i:
                    step(i, s0 + i * 2, False)
                step(UP - 1, s0 + 2 * (UP - 1), True)
                s1 = s0 + 2 * UP
                with act.Fori(0, (UP - 3) // 2) as i:
                    split(L, s1 + i * 2 + 2, a, hid[:, ds(i * 4 + 4, 2), :], [(h_ready, G + i * 2 + 3)])
                    split(L, s1 + i * 2 + 3, 1 - a, hid[:, ds(i * 4 + 6, 2), :], [(h_ready, G + i * 2 + 4)])
                split(L, s1 + UP - 1, a, hid[:, FT - 2:FT, :], [(h_ready, G + UP)])

            for credited in (s_exp, gate_th):
                act.sem_inc(credited, CREDIT)
            act.wait_ge(lam_sum, 1)
            act.activation(lexp[:, :], lsum[:, :], ACT.Exp).then_inc(lam_exp, 1)
            act.wait_ge(x_in, 16 * KT)
            act.wait_ge(params, 1)
            act.wait_ge(cleared, 3)
            with act.Fori(0, DEPTH) as L:
                split(L, 0, 0, first=True)
                split(L, 1, 1, first=True)
                ffn(L, 0, 0, 0)
                split(L, M0, 1)
                post(L, 0)
                split(L, M0 + 1, 0)
                pre(L, 1)

                def qk(A, hh):
                    act.wait_ge(z_ready, A * 2 + 2)
                    if hh:
                        act.wait_ge(s_ready, A * 8 + 4)
                    act.activation(qh[:, :], zq[:, hh, :], ACT.Copy)
                    act.activation(kh[0:HD, 0, :], zk[0:HD, hh, :], ACT.Copy)
                    act.activation(kh[HD:P, 1, :], zk[HD:P, hh, :], ACT.Copy).then_inc(q_hi, 1)

                def softmax(A, j):
                    act.wait_ge(s_max, A * 8 + j + 1)
                    for c in range(2):
                        act.activation(pm[:, c, :], PS[:, SC + c, :], ACT.Exp, bias=nmx[:, j % 2, c:c + 1], scale=SCALE,
                                       accum_out=psums[:, j % 2, c:c + 1]).then_inc(s_exp, 1)

                def a_evac(A, j):
                    act.wait_ge(a_tr, A * 8 + j + 1)
                    if j % 4 == 0:
                        act.wait_ge(pv, A * 2 + j // 4 + CREDIT)
                    act.activation(aT[:, 0, :, (j % 4) * P:(j % 4 + 1) * P],
                                   PS[:, TR, :].rearrange("p (k q) -> p k q", q=P), ACT.Copy).then_inc(a_hi, 1)

                def v_split(i, s):
                    act.wait_ge(w_used, L * STAGES + s + 1)
                    for t in range(TT):
                        ins = act.activation(vh[:, t, :, :], PS[:, t // 2, (t % 2) * 256:(t % 2 + 1) * 256]
                                             .rearrange("p (h d) -> p h d", d=P), ACT.Copy, scale=rtall[:, t:t + 1])
                    ins.then_inc(v_hi, 1)

                def o_evac(A, i, hh):
                    act.wait_ge(pv, A * 2 + hh + 1 + CREDIT)
                    act.activation(sq[:, 1, :], PS[:, OB, :], ACT.Square)
                    act.activation(hid[:, ds(i * 2 + 8 + hh, 1), :], PS[:, OB, :].unsqueeze(1), ACT.Copy).then_inc(o_sq, 1)

                def attend(i):
                    A = L * PAIRS + i
                    s = M0 + i * ATT + 3
                    softmax(A, 0)
                    softmax(A, 1)
                    a_evac(A, 0)
                    softmax(A, 2)
                    a_evac(A, 1)
                    softmax(A, 3)
                    qk(A, 1)
                    split(L, s + 2, (M0 + 3) % 2)
                    a_evac(A, 2)
                    softmax(A, 4)
                    a_evac(A, 3)
                    softmax(A, 5)
                    o_evac(A, i, 0)
                    a_evac(A, 4)
                    softmax(A, 6)
                    split(L, s + 3, M0 % 2)
                    a_evac(A, 5)
                    softmax(A, 7)
                    a_evac(A, 6)
                    split(L, s + 4, (M0 + 1) % 2)
                    a_evac(A, 7)
                    o_evac(A, i, 1)

                split(L, M0 + 2, M0 % 2)
                rms(L, 1)
                split(L, M0 + 3, (M0 + 1) % 2)
                qk(L * PAIRS, 0)
                v_split(0, M0 + 2)
                split(L, M0 + 4, M0 % 2)
                with act.Fori(0, PAIRS - 1) as i:
                    attend(i)
                    s = M0 + i * ATT + ATT
                    split(L, s + 2, M0 % 2)
                    split(L, s + 3, (M0 + 1) % 2)
                    qk(L * PAIRS + i + 1, 0)
                    v_split(i + 1, s + 2)
                    split(L, s + 4, M0 % 2)
                attend(PAIRS - 1)

                def gate(n, g, t, dst):
                    act.wait_ge(gate_z, L * 8 + 4 * g + t + 1)
                    for j in range(2):
                        ins = act.activation(dst[:, j, :], gatez[:, j, :], ACT.Tanh, scale=0.5,
                                             bias=bg[:, ds(L, 1), g, 2 * t + j])
                    ins.then_inc(gate_th, 1)

                for t in range(4):
                    if t < 2:
                        split(L, GC0 + t + 2, (GC0 + t) % 2)
                    else:
                        split(L, GC0 + t + 2, (GC0 + t) % 2, hid[:, 2 * t - 4:2 * t - 2, :], [(conv_done, L * PAIRS + t - 1)])
                    gate(GC0, 0, t, yw[:, 2 * t:2 * t + 2, :])
                for t in range(4):
                    if t < 2:
                        split(L, CO0 + t + 2, (CO0 + t) % 2, hid[:, 2 * t + 4:2 * t + 6, :], [(conv_done, L * PAIRS + t + 3)])
                    else:
                        split(L, CO0 + t + 2, (CO0 + t) % 2, hid[:, 2 * t + 4:2 * t + 6, :], [(o_done, L * HEADS + 2 * t - 2 + CREDIT)])
                for t in range(2):
                    split(L, AO0 + t + 2, (AO0 + t) % 2, hid[:, 2 * t + 12:2 * t + 14, :], [(o_done, L * HEADS + 2 * t + 6 + CREDIT)])
                split(L, AO0 + 4, AO0 % 2)
                for m in range(KT):
                    act.wait_ge(y_ready, L * (5 * KT) + 2 * KT + m + 1)
                    act.activation(hid[:, 8 + m, :], PS[:, m, :], ACT.Copy, scale=0.5).then_inc(ao_read, 1)
                split(L, AO0 + 5, (AO0 + 1) % 2)
                for t in range(4):
                    if t < 2:
                        split(L, GA0 + t + 2, (GA0 + t) % 2)
                    else:
                        split(L, GA0 + t + 2, (GA0 + t) % 2, hid[:, 2 * t - 4:2 * t - 2, :], [(m_ready, L * 4 + t - 1)])
                    gate(GA0, 1, t, gateth)
                for t in range(3):
                    if t < 2:
                        split(L, WO0 + t + 2, (WO0 + t) % 2, hid[:, 2 * t + 4:2 * t + 6, :], [(m_ready, L * 4 + t + 3)])
                    else:
                        split(L, F20, F20 % 2)
                post(L, 1)
                split(L, F20 + 1, (F20 + 1) % 2)
                ffn(L, 1, F20, 2)
                post(L, 2)

        @block.tensor
        def _(pe):
            pe.wait_ge(consts_in, 16 * 9)
            pe.wait_ge(cleared, 3)
            pe.sem_inc(pv, CREDIT)

            def product(bank, slot, off, xhi, xlo, start, stop):
                hi, lo = wh[:, slot, off:off + P], wl[:, slot, off:off + P]
                pe.matmul(PS[:, bank, :], hi, xhi, start=start, stop=False)
                pe.matmul(PS[:, bank, :], hi, xlo, start=False, stop=False)
                return pe.matmul(PS[:, bank, :], lo, xhi, start=False, stop=stop)

            def wide_ops(L, s, slot, ordinal, banks, norm=None):
                def step(k, j):
                    def run():
                        if k == 0 and j == 0:
                            pe.wait_ge(w_lo, L * STAGES + s + (RAW_CREDIT + 1))
                            pe.wait_ge(wide_read, L * WIDE + ordinal + (READ_CREDIT - 1))
                        if norm is not None and j == 0:
                            pe.wait_ge(xw_ready, L * (3 * KT) + norm * KT + k + 1)
                        mm = product(banks + j, slot, k * 256 + j * P, xh[:, k, :], xl[:, k, :], k == 0, k == KT - 1)
                        if k == KT - 1 and j == 1:
                            mm.then_inc(w_used, 1)
                    return run
                return [step(k, j) for k in range(KT) for j in range(2)]

            def wide_stage(*a, **kw):
                for op in wide_ops(*a, **kw):
                    op()

            def norm_stat(L, n):
                pe.wait_ge(acc_done, L * 36 + n * 6 + 6)
                for t in range(TT):
                    pe.matmul(PS[:, 4, t:t + 1], acc[:, t * P:(t + 1) * P], ones[:, 0:1], start=(t == 0), stop=False,
                              skip_group_check=True)
                pe.wait_ge(sq_ready, L * (6 * KT) + n * KT + KT)
                for t in range(TT):
                    mm = pe.matmul(PS[:, 4, t:t + 1], sq[:, 1, t * P:(t + 1) * P], ones[:, 0:1], start=False,
                                   stop=(t == TT - 1), skip_group_check=True)
                mm.then_inc(stat, 1)

            def norm_wide(L, n):
                pe.wait_ge(diag_ready, L * 6 + n + 1)
                pe.matmul(PS[:, 5, :], ones[:, :], diag[:, :, :], start=True, stop=True).then_inc(wide, 1)

            def first_pair(L, s, ordinal, n):
                a, b = (wide_ops(L, s + q, (s + q) % 2, ordinal + q, 2 * q, norm=n) for q in range(2))

                def go(ops):
                    ops.pop(0)()
                    ops.pop(0)()
                for k in range(KT):
                    go(a)
                    if k % 2:
                        go(b)
                go(b)
                norm_stat(L, 2 * n)
                go(b)
                go(b)
                norm_wide(L, 2 * n)
                go(b)

            def deep_stage(L, s, slot, first, last, bank_free=None, y=None):
                pe.wait_ge(w_lo, L * STAGES + s + (RAW_CREDIT + 1))
                for m in (list(range(KT)) if last or bank_free is None else [4, 5, 6, 7, 0, 1, 2, 3]):
                    if bank_free is not None:
                        bank_free(m)
                    for kk in range(2):
                        mm = product(m, slot, kk * D + m * P, jit[:, slot, 0, kk, :], jit[:, slot, 1, kk, :],
                                     first and kk == 0, last and kk == 1)
                    if last:
                        mm.then_inc(y_ready, 1)
                if last:
                    pe.drain()
                    pe.sem_inc(w_used, 1)
                else:
                    mm.then_inc(w_used, 1)

            def ffn(L, s0, ordinal, n):
                a = s0 % 2
                first_pair(L, s0, ordinal, n)
                with pe.Fori(1, UP) as i:
                    wide_stage(L, s0 + i * 2, a, ordinal + i * 2, 0)
                    wide_stage(L, s0 + i * 2 + 1, 1 - a, ordinal + i * 2 + 1, 2)
                s1 = s0 + 2 * UP

                def free(m):
                    if m == 0:
                        pe.wait_ge(wide_read, L * WIDE + ordinal + 2 * UP + READ_CREDIT)
                deep_stage(L, s1, a, True, False, free)
                with pe.Fori(0, (UP - 3) // 2 + 0) as i:
                    deep_stage(L, s1 + i * 2 + 1, 1 - a, False, False)
                    deep_stage(L, s1 + i * 2 + 2, a, False, False)
                deep_stage(L, s1 + UP - 2, 1 - a, False, False)
                deep_stage(L, s1 + UP - 1, a, False, True)
                norm_stat(L, 2 * n + 1)
                norm_wide(L, 2 * n + 1)

            with pe.Fori(0, DEPTH) as L:
                ffn(L, 0, 0, 0)
                o0 = 2 * UP
                o1 = o0 + ATT * PAIRS
                first_pair(L, M0, o0, 1)

                def v_ops(L, s, slot, ordinal):
                    def step(t, k0):
                        def run():
                            if t == 0 and k0 == 0:
                                pe.wait_ge(w_lo, L * STAGES + s + (RAW_CREDIT + 1))
                                pe.wait_ge(wide_read, L * WIDE + ordinal + (READ_CREDIT - 1))
                            o = PS[:, t // 2, (t % 2) * 256:(t % 2 + 1) * 256]
                            for k in (k0, k0 + 1):
                                hi, lo = (w[:, slot, k * 256:(k + 1) * 256] for w in (wh, wl))
                                pe.matmul(o, xh[:, k, t * P:(t + 1) * P], hi, start=(k == 0), stop=False)
                                pe.matmul(o, xh[:, k, t * P:(t + 1) * P], lo, start=False, stop=False)
                                mm = pe.matmul(o, xl[:, k, t * P:(t + 1) * P], hi, start=False, stop=(k == KT - 1))
                            if t == TT - 1 and k0 == KT - 2:
                                mm.then_inc(w_used, 1)
                        return run
                    return [step(t, k0) for t in range(TT) for k0 in range(0, KT, 2)]

                def stage_ops(i, n):
                    s, slot, o = M0 + i * ATT + n, (M0 + n) % 2, o0 + i * ATT + n
                    return v_ops(L, s, slot, o) if n == 2 else wide_ops(L, s, slot, o, 2 * (n % 2))

                def work(flow, n):
                    for _ in range(n):
                        flow.pop(0)()

                def scores(A, j):
                    hh, qt = j // 4, j % 4
                    if qt == 0:
                        pe.wait_ge(qk_lo, A * 2 + hh + 1)
                    pe.wait_ge(s_exp, A * 16 + 2 * j + CREDIT)
                    q = slice(qt * P, (qt + 1) * P)
                    for c in range(2):
                        pe.matmul(PS[:, SC + c, :], qh[:, q], kh[:, c, :], start=True, stop=False)
                        pe.matmul(PS[:, SC + c, :], qh[:, q], kl[:, c, :], start=False, stop=False)
                        mm = pe.matmul(PS[:, SC + c, :], ql[:, q], kh[:, c, :], start=False, stop=True)
                    mm.then_inc(s_ready, 1)

                def a_transpose(A, j):
                    pe.wait_ge(a_ready, A * 8 + j + 1)
                    pe.wait_ge(a_lo, A * 8 + j + CREDIT)
                    for kt in range(TT):
                        mm = pe.transpose(PS[:, TR, kt * P:(kt + 1) * P], att[:, j % 2, kt * P:(kt + 1) * P], ident[:, :])
                    mm.then_inc(a_tr, 1)

                def values(A, hh):
                    pe.wait_ge(a_lo, A * 8 + 4 * hh + 4 + CREDIT)
                    pe.wait_ge(v_lo, A + 1)
                    pe.wait_ge(o_done, A * 2 + hh + CREDIT)
                    for kt in range(TT):
                        pe.matmul(PS[:, OB, :], vh[:, kt, hh, :], aT[:, 0, kt, :], start=(kt == 0), stop=False)
                        pe.matmul(PS[:, OB, :], vh[:, kt, hh, :], aT[:, 1, kt, :], start=False, stop=False)
                        mm = pe.matmul(PS[:, OB, :], vl[:, kt, hh, :], aT[:, 0, kt, :], start=False, stop=(kt == TT - 1))
                    mm.then_inc(pv, 1)

                def out_stat(A, hh):
                    pe.wait_ge(o_sq, A * 2 + hh + 1)
                    for t in range(TT):
                        mm = pe.matmul(PS[:, OB, t:t + 1], sq[:, 1, t * P:(t + 1) * P], ones[:, 0:1], start=True, stop=True)
                    mm.then_inc(o_stat, 1)

                def out_wide(A, hh):
                    pe.wait_ge(o_diag, A * 2 + hh + 1)
                    pe.matmul(PS[:, OB, :], ones[:, :], diag[:, :, :], start=True, stop=True).then_inc(o_wide, 1)

                def attend(i):
                    A = L * PAIRS + i
                    flow = stage_ops(i, 3) + stage_ops(i, 4) + stage_ops(i, 5)
                    for j in range(8):
                        scores(A, j)
                        work(flow, 6)
                        if j == 5:
                            values(A, 0)
                        if j == 6:
                            out_stat(A, 0)
                        if j == 7:
                            out_wide(A, 0)
                        if j:
                            a_transpose(A, j - 1)

                def tail(i, flow):
                    A = L * PAIRS + i
                    work(flow, 3)
                    a_transpose(A, 7)
                    work(flow, 5)
                    values(A, 1)
                    work(flow, 3)
                    out_stat(A, 1)
                    work(flow, 5)
                    out_wide(A, 1)
                    work(flow, len(flow))

                work(v := stage_ops(0, 2), len(v))
                with pe.Fori(0, PAIRS - 1) as i:
                    attend(i)
                    tail(i, stage_ops(i + 1, 0) + stage_ops(i + 1, 1) + stage_ops(i + 1, 2))
                attend(PAIRS - 1)
                tail(PAIRS - 1, [op for t in range(4) for op in
                                 wide_ops(L, GC0 + t, (GC0 + t) % 2, o1 + t, 2 * (t % 2))])
                for t in range(4):
                    def gates_read(m):
                        if m == 0:
                            pe.wait_ge(wide_read, L * WIDE + o1 + 4 + READ_CREDIT)
                        if m == 4:
                            pe.wait_ge(o_done, L * HEADS + HEADS + CREDIT)
                    deep_stage(L, CO0 + t, (CO0 + t) % 2, t == 0, t == 3, gates_read if t == 0 else None)
                for t in range(4):
                    def conv_read(m):
                        pe.wait_ge(co_read, L * KT + (m + 1 if m < 4 else 8))
                    deep_stage(L, AO0 + t, (AO0 + t) % 2, t == 0, t == 3, conv_read if t == 0 else None)
                pe.wait_ge(ao_read, L * KT + KT)
                for t in range(4):
                    wide_stage(L, GA0 + t, (GA0 + t) % 2, o1 + 4 + t, 2 * (t % 2))
                for t in range(4):
                    def gates_read2(m):
                        if m == 0:
                            pe.wait_ge(wide_read, L * WIDE + o1 + 8 + READ_CREDIT)
                    deep_stage(L, WO0 + t, (WO0 + t) % 2, t == 0, t == 3, gates_read2 if t == 0 else None)
                norm_stat(L, 3)
                norm_wide(L, 3)
                ffn(L, F20, o1 + 8, 2)

        @block.vector
        def _(dve):
            for _ in range(RAW_CREDIT):
                dve.memset(rv[:, :], 0.0).then_inc(w_lo, 1)
                dve.drain()
            for credited in (a_lo, o_done, x_ready):
                dve.sem_inc(credited, CREDIT)
            for _ in range(READ_CREDIT):
                dve.drain()
                dve.memset(rv[:, :], 0.0).then_inc(wide_read, 1)
            dve.wait_ge(consts_in, 16 * 9)
            for n in (1, 5):
                dve.tensor_scalar(nw[:, :, n, :], nw[:, :, n, :], 0.5, None, ALU.mult)
            dve.tensor_scalar(bg[:, :, :, :], bg[:, :, :, :], 0.5, None, ALU.mult)
            dve.tensor_tensor(sub[:, :], sub[:, :], lamc[:, 1, :], ALU.mult)
            lv = lamv.rearrange("p (l a b d) -> p (l a) b d", l=DEPTH, a=2, b=2)
            prod = hid[:, 1, 0:DEPTH * 2 * HD].rearrange("p (l d) -> p l d", d=HD)
            dve.tensor_tensor(prod, lv[:, :, 0, :], lv[:, :, 1, :], ALU.mult)
            dve.drain()
            dve.tensor_reduce(lsum[:, :], prod, AX.X, ALU.add).then_inc(lam_sum, 1)
            dve.wait_ge(lam_exp, 1)
            le = lexp[:, :].rearrange("p (l a) -> p l a", a=2)
            dve.tensor_tensor(nlam[:, :], le[:, :, 1], le[:, :, 0], ALU.subtract)
            dve.drain()
            dve.tensor_tensor(nlam[:, :], nlam[:, :], lamc[:, 0, :], ALU.subtract).then_inc(params, 1)
            dve.drain()

            def rsqrt(bank_cols, count, done):
                dve.tensor_scalar(rv[:, :], bank_cols, 1.0 / count, EPS, ALU.mult, ALU.add)
                dve.drain()
                dve.tensor_scalar(rt[:, :].bitcast(i32), rv[:, :].bitcast(i32), 1, None, ALU.logical_shift_right)
                dve.drain()
                dve.tensor_scalar(ry[:, :].bitcast(i32), rt[:, :].bitcast(i32), -1.0, float(0x5F3759DF), ALU.mult, ALU.add)
                for _ in range(3):
                    dve.drain()
                    dve.tensor_tensor(rt[:, :], ry[:, :], ry[:, :], ALU.mult)
                    dve.drain()
                    dve.scalar_tensor_tensor(out=rt[:, :], in0=rt[:, :], scalar=-0.5, in1=rv[:, :], op0=ALU.mult, op1=ALU.mult)
                    dve.drain()
                    dve.scalar_tensor_tensor(out=ry[:, :], in0=rt[:, :], scalar=1.5, in1=ry[:, :], op0=ALU.add, op1=ALU.mult)
                dve.drain()
                dve.tensor_tensor(diag[:, :, :], ident[:, :].unsqueeze(1).to_broadcast([P, TT, P]),
                                  ry[:, :].unsqueeze(2).to_broadcast([P, TT, P]), ALU.mult).then_inc(done, 1)
                dve.drain()

            def split(L, s, slot, src=None):
                dve.wait_ge(w_hi, L * STAGES + s + 1)
                if src is not None:
                    dve.tensor_tensor(jit[:, slot, 1, :, :], src, jit[:, slot, 0, :, :].bitcast(f32), ALU.subtract)
                dve.tensor_tensor(wl[:, slot, :], raw[:, slot, :], wh[:, slot, :].bitcast(f32), ALU.subtract).then_inc(w_lo, 1)

            def x_lo(L, n, k):
                dve.wait_ge(x_hi, L * (3 * KT) + n * KT + k + 1)
                dve.scalar_tensor_tensor(out=xl[:, k, :], in0=x[:, k, :], scalar=nw[:, ds(L, 1), 2 * n, k],
                                         in1=xh[:, k, :].bitcast(f32), op0=ALU.mult, op1=ALU.subtract).then_inc(xw_ready, 1)

            def pre_rms(L, n):
                dve.wait_ge(stat, L * 6 + 2 * n + 1)
                rsqrt(PS[:, 4, 0:TT], D, diag_ready)

            def post(L, n, s=None):
                dve.wait_ge(stat, L * 6 + 2 * n + 2)
                rsqrt(PS[:, 4, 0:TT], D, diag_ready)
                dve.wait_ge(wide, L * 6 + 2 * n + 2)
                dve.wait_ge(y_scaled, L * (3 * KT) + n * KT + KT)
                for k in range(KT):
                    dve.tensor_tensor(yw[:, k, :], PS[:, 5, :], yw[:, k, :], ALU.mult)
                    dve.drain()
                    dve.tensor_tensor(x[:, k, :], x[:, k, :], yw[:, k, :], ALU.add).then_inc(x_ready, 1)
                    if k == 1 and s is not None:
                        split(L, s, s % 2)
                    if k and n < 2:
                        x_lo(L, n + 1, k - 1)
                if n < 2:
                    x_lo(L, n + 1, KT - 1)

            def rows(t):
                return t.unsqueeze(1).to_broadcast([P, 2, T])

            def scaled(dst, bank, done):
                dve.tensor_tensor(dst, PS[:, bank:bank + 2, :], rows(rpre[:, :]), ALU.mult).then_inc(done, 1)

            def used(L, s):
                dve.wait_ge(w_used, L * STAGES + s + 1)

            def ffn(L, w, s0, n):
                a = s0 % 2
                G = (L * 2 + w) * UP
                pre_rms(L, n)
                split(L, s0 + 2, a)

                def step(i, s, last, first=False):
                    used(L, s)
                    dve.wait_ge(r_ready, L * 3 + n + 1)
                    scaled(gz, 0, wide_read)
                    dve.drain()
                    dve.sem_inc(gz_ready, 1)
                    if not first:
                        split(L, s + 2, a, hid[:, 0:2, :] if last else None)
                    used(L, s + 1)
                    scaled(uz, 2, wide_read)
                    split(L, s + 3, 1 - a, hid[:, 2:4, :] if last else None)
                    dve.wait_ge(th_ready, G + i + 1)
                    dve.scalar_tensor_tensor(out=gz, in0=th, scalar=1.0, in1=gz, op0=ALU.add, op1=ALU.mult)
                    dve.drain()
                    dve.scalar_tensor_tensor(out=hid[:, ds(i * 2, 2), :], in0=gz, scalar=0.5, in1=uz,
                                             op0=ALU.mult, op1=ALU.mult).then_inc(h_ready, 1)
                    dve.drain()

                step(0, s0, False, first=True)
                with dve.Fori(1, UP - 1) as i:
                    step(i, s0 + i * 2, False)
                step(UP - 1, s0 + 2 * (UP - 1), True)
                s1 = s0 + 2 * UP
                with dve.Fori(0, (UP - 3) // 2) as i:
                    split(L, s1 + i * 2 + 2, a, hid[:, ds(i * 4 + 4, 2), :])
                    split(L, s1 + i * 2 + 3, 1 - a, hid[:, ds(i * 4 + 6, 2), :])
                split(L, s1 + UP - 1, a, hid[:, FT - 2:FT, :])

            with dve.Fori(0, DEPTH) as L:
                split(L, 0, 0)
                split(L, 1, 1)
                for k in range(KT):
                    x_lo(L, 0, k)
                ffn(L, 0, 0, 0)
                split(L, M0, 1)
                post(L, 0, M0 + 1)

                def rope(z, bank, after):
                    scaled(z, bank, wide_read)
                    after()
                    dve.drain()
                    dve.stream_shuffle(shuf, z, list(range(8, 16)) + list(range(8)) + list(range(16, 32)))
                    dve.drain()
                    dve.tensor_tensor(shuf, shuf, rows(sinT[:, :]), ALU.mult)
                    dve.tensor_tensor(z, z, rows(cosT[:, :]), ALU.mult)
                    dve.drain()
                    dve.tensor_tensor(z, z, shuf, ALU.add).then_inc(z_ready, 1)
                    dve.drain()

                def qk(A, hh):
                    dve.wait_ge(q_hi, A * 2 + hh + 1)
                    dve.tensor_tensor(ql[:, :], zq[:, hh, :], qh[:, :].bitcast(f32), ALU.subtract)
                    dve.tensor_tensor(kl[0:HD, 0, :], zk[0:HD, hh, :], kh[0:HD, 0, :].bitcast(f32), ALU.subtract)
                    dve.tensor_tensor(kl[HD:P, 1, :], zk[HD:P, hh, :], kh[HD:P, 1, :].bitcast(f32), ALU.subtract) \
                       .then_inc(qk_lo, 1)

                def row_max(A, j):
                    dve.wait_ge(s_ready, A * 8 + j + 1)
                    dve.tensor_reduce(mx[:, :], PS[:, SC:SC + 2, :], AX.X, ALU.max)
                    dve.drain()
                    dve.tensor_scalar(nmx[:, j % 2, :], mx[:, :], -SCALE, None, ALU.mult).then_inc(s_max, 1)

                def combine(A, j):
                    dve.wait_ge(s_exp, A * 16 + 2 * j + 2 + CREDIT)
                    dve.reciprocal(rsum[:, :], psums[:, j % 2, :])
                    dve.drain()
                    if j >= 2:
                        dve.wait_ge(a_tr, A * 8 + j - 1)
                    dve.tensor_scalar(att[:, j % 2, :], pm[:, 1, :], rsum[:, 1:2], nlam[:, ds(L, 1)], ALU.mult, ALU.mult)
                    dve.drain()
                    dve.scalar_tensor_tensor(out=att[:, j % 2, :], in0=pm[:, 0, :], scalar=rsum[:, 0:1], in1=att[:, j % 2, :],
                                             op0=ALU.mult, op1=ALU.add).then_inc(a_ready, 1)

                def a_evac(A, j):
                    dve.wait_ge(a_hi, A * 8 + j + 1)
                    sl = slice((j % 4) * P, (j % 4 + 1) * P)
                    dve.tensor_tensor(aT[:, 1, :, sl], PS[:, TR, :].rearrange("p (k q) -> p k q", q=P),
                                      aT[:, 0, :, sl].bitcast(f32), ALU.subtract).then_inc(a_lo, 1)

                def v_split(A):
                    dve.wait_ge(v_hi, A + 1)
                    for t in range(TT):
                        ins = dve.scalar_tensor_tensor(
                            out=vl[:, t, :, :], in0=PS[:, t // 2, (t % 2) * 256:(t % 2 + 1) * 256].rearrange("p (h d) -> p h d", d=P),
                            scalar=rtall[:, t:t + 1], in1=vh[:, t, :, :].bitcast(f32), op0=ALU.mult, op1=ALU.subtract)
                    ins.then_inc(v_lo, 1)

                def out_norm(A, hh):
                    dve.wait_ge(o_stat, A * 2 + hh + 1)
                    rsqrt(PS[:, OB, 0:TT], P, o_diag)

                def out_scale(A, i, hh):
                    dve.wait_ge(o_wide, A * 2 + hh + 1)
                    o = hid[:, ds(i * 2 + 8 + hh, 1), :]
                    dve.scalar_tensor_tensor(out=o, in0=o, scalar=sub[:, ds(L, 1)], in1=PS[:, OB, :].unsqueeze(1),
                                             op0=ALU.mult, op1=ALU.mult).then_inc(o_done, 1)

                def conv(i):
                    yc2 = hid[:, ds(i * 2, 2), :]
                    dve.tensor_tensor(cu, cu, yc2, ALU.mult)
                    dve.drain()
                    for n in (1, 0, 2):
                        for hh in range(2):
                            w3 = cw[:, ds(L, 1), n, ds(i * 2 + hh, 1)]
                            u = cu[:, hh:hh + 1, :]
                            yc = hid[:, ds(i * 2 + hh, 1), :]
                            if n == 1:
                                dve.tensor_scalar(yc, u, w3, None, ALU.mult)
                                continue
                            to, of = (slice(1, T), slice(0, T - 1)) if n == 0 else (slice(0, T - 1), slice(1, T))
                            dve.scalar_tensor_tensor(out=yc[:, :, to], in0=u[:, :, of], scalar=w3, in1=yc[:, :, to],
                                                     op0=ALU.mult, op1=ALU.add)
                        dve.drain()
                    dve.tensor_tensor(yc2, yc2, convb, ALU.mult).then_inc(conv_done, 1)
                    dve.drain()

                def qkv(i, first=False):
                    A, s = L * PAIRS + i, M0 + i * ATT
                    used(L, s)
                    if first:
                        split(L, s + 2, M0 % 2)
                        dve.wait_ge(r_ready, L * 3 + 2)
                    rope(zq, 0, lambda: None if first else split(L, s + 2, M0 % 2))
                    used(L, s + 1)
                    rope(zk, 2, lambda: split(L, s + 3, (M0 + 1) % 2))
                    qk(A, 0)
                    used(L, s + 2)
                    v_split(A)
                    dve.drain()
                    dve.sem_inc(wide_read, 1)
                    split(L, s + 4, M0 % 2)

                def attend(i):
                    A, s = L * PAIRS + i, M0 + i * ATT + 3
                    row_max(A, 0)
                    combine(A, 0)
                    row_max(A, 1)
                    combine(A, 1)
                    row_max(A, 2)
                    a_evac(A, 0)
                    combine(A, 2)
                    row_max(A, 3)
                    a_evac(A, 1)
                    combine(A, 3)
                    qk(A, 1)
                    used(L, s)
                    scaled(convb, 2, wide_read)
                    row_max(A, 4)
                    a_evac(A, 2)
                    combine(A, 4)
                    split(L, s + 2, (M0 + 3) % 2)
                    row_max(A, 5)
                    a_evac(A, 3)
                    combine(A, 5)
                    row_max(A, 6)
                    a_evac(A, 4)
                    combine(A, 6)
                    used(L, s + 1)
                    scaled(hid[:, ds(i * 2, 2), :], 0, wide_read)
                    out_norm(A, 0)
                    row_max(A, 7)
                    a_evac(A, 5)
                    combine(A, 7)
                    out_scale(A, i, 0)
                    split(L, s + 3, M0 % 2)
                    a_evac(A, 6)
                    used(L, s + 2)
                    scaled(cu, 2, wide_read)
                    split(L, s + 4, (M0 + 1) % 2)
                    a_evac(A, 7)
                    dve.drain()
                    conv(i)
                    out_norm(A, 1)
                    out_scale(A, i, 1)

                pre_rms(L, 1)
                dve.tensor_copy(rtall[:, :], ry[:, :])
                qkv(0, first=True)
                with dve.Fori(0, PAIRS - 1) as i:
                    attend(i)
                    qkv(i + 1)
                attend(PAIRS - 1)

                for t in range(4):
                    used(L, GC0 + t)
                    dve.wait_ge(gate_th, L * 8 + t + CREDIT)
                    scaled(gatez, 2 * (t % 2), wide_read)
                    dve.drain()
                    dve.sem_inc(gate_z, 1)
                    if t < 2:
                        split(L, GC0 + t + 2, (GC0 + t) % 2)
                    else:
                        split(L, GC0 + t + 2, (GC0 + t) % 2, hid[:, 2 * t - 4:2 * t - 2, :])
                for t in range(3):
                    split(L, CO0 + t + 2, (CO0 + t) % 2, hid[:, 2 * t + 4:2 * t + 6, :])
                dve.wait_ge(gate_th, L * 8 + 4 + CREDIT)
                for m in range(KT):
                    dve.wait_ge(y_ready, L * (5 * KT) + KT + m + 1)
                    dve.scalar_tensor_tensor(out=hid[:, m, :], in0=yw[:, m, :], scalar=1.0, in1=PS[:, m, :],
                                             op0=ALU.add, op1=ALU.mult).then_inc(co_read, 1)
                split(L, CO0 + 5, (CO0 + 3) % 2, hid[:, 10:12, :])
                for t in range(4):
                    if t < 2:
                        split(L, AO0 + t + 2, (AO0 + t) % 2, hid[:, 2 * t + 12:2 * t + 14, :])
                    else:
                        split(L, AO0 + t + 2, (AO0 + t) % 2)
                dve.wait_ge(ao_read, L * KT + KT)
                for t in range(4):
                    used(L, GA0 + t)
                    scaled(gatez, 2 * (t % 2), wide_read)
                    dve.drain()
                    dve.sem_inc(gate_z, 1)
                    if t < 2:
                        split(L, GA0 + t + 2, (GA0 + t) % 2)
                    else:
                        split(L, GA0 + t + 2, (GA0 + t) % 2, hid[:, 2 * t - 4:2 * t - 2, :])
                    dve.wait_ge(gate_th, L * 8 + 5 + t + CREDIT)
                    dve.scalar_tensor_tensor(out=gateth, in0=gateth, scalar=1.0, in1=hid[:, 8 + 2 * t:10 + 2 * t, :],
                                             op0=ALU.add, op1=ALU.mult)
                    dve.drain()
                    dve.scalar_tensor_tensor(out=hid[:, 2 * t:2 * t + 2, :], in0=hid[:, 2 * t:2 * t + 2, :], scalar=0.5,
                                             in1=gateth, op0=ALU.mult, op1=ALU.add).then_inc(m_ready, 1)
                    dve.drain()
                for t in range(3):
                    if t < 2:
                        split(L, WO0 + t + 2, (WO0 + t) % 2, hid[:, 2 * t + 4:2 * t + 6, :])
                    else:
                        split(L, F20, F20 % 2)
                post(L, 1, F20 + 1)
                ffn(L, 1, F20, 2)
                post(L, 2)


def rope_tables():
    rot = HD // 4
    half = rot // 2
    inv = (np.float32(500000.0) ** (-np.arange(0, rot, 2, dtype=np.float32) / np.float32(rot))).astype(np.float32)
    ang = np.arange(T, dtype=np.float32)[None, :] * inv[:, None]
    cos, sin = np.cos(ang).astype(np.float32), np.sin(ang).astype(np.float32)
    C, S = np.ones((P, T), np.float32), np.zeros((P, T), np.float32)
    for base in (0, HD):
        C[base:base + half], C[base + half:base + rot] = cos, cos
        S[base:base + half], S[base + half:base + rot] = -sin, sin
    return C, S


def kernel(**inputs):
    import concourse.bacc as _bacc
    from concourse.bass_utils import run_bass_kernel_spmd as _run

    a = {k: np.asarray(v) for k, v in inputs.items()}
    C, S = rope_tables()
    init = [0.8 - 0.6 * math.exp(-0.3 * l) for l in range(DEPTH)]
    lam_const = np.broadcast_to(np.array(init + [1.0 - v for v in init], np.float32), (P, 2 * DEPTH))

    def columns(v):
        return v.reshape(-1, P).T

    arrays = {
        "xT": a["x"][0].T, "w_in": a["w_in"], "w_conv_out": a["w_conv_out"], "w_attn_out": a["w_attn_out"],
        "w_o": a["w_o"], "ffn1_w13": a["ffn1_w13"], "ffn1_w2": a["ffn1_w2"], "ffn2_w13": a["ffn2_w13"],
        "ffn2_w2": a["ffn2_w2"], "norm_wT": columns(a["norm_w"]), "b_gateT": columns(a["b_gate"]),
        "conv_wT": columns(a["conv_w"]), "sublnT": columns(a["subln_w"]), "lam_vec": a["lam_vec"],
        "ropeC": C, "ropeS": S, "ident_in": np.eye(P, dtype=np.float32), "lam_const": lam_const,
    }
    arrays = {f"in_{k}": np.ascontiguousarray(v) for k, v in arrays.items()}
    nc = _bacc.Bacc("TRN2", target_bir_lowering=False, num_devices=1)
    args = [nc.dram_tensor(k, v.shape, mybir.dt.from_np(v.dtype), kind="ExternalInput").ap() for k, v in arrays.items()]
    out = nc.dram_tensor("out_0", (D, T), mybir.dt.float32, kind="ExternalOutput").ap()
    encoder_kernel(nc, *args, out)
    r = _run(nc, [arrays], core_ids=[0])
    return np.ascontiguousarray(r.results[0]["out_0"].T)[None]
```

```python
import math

import numpy as np
import concourse.bass as bass
from concourse import mybir
from contextlib import ExitStack

DEPTH = 2
D = 1024
T = 512
DFF = 2816
HEADS = 8
P = 128
KT = D // P
FT = DFF // P
UP = FT // 2
TT = T // P
HD = 64
ROWS = (slice(0, HD), slice(HD, P))
EPS = 1e-6
SCALE = HD ** -0.5
STAGE = 2048

FFN = 2 * UP + UP
PAIRS = HEADS // 2
ATT = 6
MIX = ATT * PAIRS + 4 * 4 + 4
STAGES = 2 * FFN + MIX
M0 = FFN
GC0 = M0 + ATT * PAIRS
CO0 = GC0 + 4
AO0 = CO0 + 4
GA0 = AO0 + 4
WO0 = GA0 + 4
F20 = M0 + MIX
WIDE = 2 * 2 * UP + ATT * PAIRS + 8
RAW_CREDIT = 2
READ_CREDIT = 2
LAST_ORDER = (0, 1, 3, 2, 5, 7, 4, 6)
POOL_SUMS = 5
CREDIT = 1


def encoder_kernel(nc, xT, w_in, w_conv_out, w_attn_out, w_o, ffn1_w13, ffn1_w2, ffn2_w13, ffn2_w2,
                   norm_wT, b_gateT, conv_wT, sublnT, lam_vec, ropeC, ropeS, ident_in, lam_const, out):
    f32, f32r, i32 = mybir.dt.float32, mybir.dt.float32r, mybir.dt.int32
    ALU, ACT, AX = mybir.AluOpType, mybir.ActivationFunctionType, mybir.AxisListType
    ds = bass.ds

    with ExitStack() as ctx:
        def sb(name, shape, dt=f32):
            return ctx.enter_context(nc.sbuf_tensor(name, shape, dt))

        def sem(name):
            return ctx.enter_context(nc.semaphore(name))

        x = sb("x", [P, KT, T])
        xh = sb("xh", [P, KT, T], f32r)
        xl = sb("xl", [P, KT, T], f32r)
        yw = sb("yw", [P, KT, T])
        hid = sb("hid", [P, FT, T])
        raw = sb("raw", [P, 2, STAGE])
        wh = sb("wh", [P, 2, STAGE], f32r)
        wl = sb("wl", [P, 2, STAGE], f32r)
        jit = sb("jit", [P, 2, 2, 2, T], f32r)
        aT = jit[:, :, :, :, :].rearrange("p a b c t -> p a (b c) t")
        khl = sb("khl", [P, 2, T], f32r)
        qhh = sb("qhh", [P, 2, T], f32r)
        ql = sb("ql", [P, 2, T], f32r)
        vh = sb("vh", [P, TT, 2, P], f32r)
        vl = sb("vl", [P, TT, 2, P], f32r)
        cosT = sb("cosT", [P, T])
        sinT = sb("sinT", [P, T])
        rpre = sb("rpre", [P, T])
        acc = sb("acc", [P, T])
        sq = sb("sq", [P, 2, T])
        ones = sb("ones", [P, P])
        ident = sb("ident", [P, P])
        nw = sb("nw", [P, DEPTH, 6, KT])
        bg = sb("bg", [P, DEPTH, 2, KT])
        cw = sb("cw", [P, DEPTH, 3, KT])
        sub = sb("sub", [P, DEPTH])
        bgh = sb("bgh", [P, DEPTH, 2, KT])
        subs = sb("subs", [P, DEPTH])
        lamc = sb("lamc", [P, 2, DEPTH])
        nlam = sb("nlam", [P, DEPTH])
        lsum = sb("lsum", [P, 2 * DEPTH])
        lexp = sb("lexp", [P, 2 * DEPTH])
        rv = sb("rv", [P, TT])
        rw = sb("rw", [P, TT])
        rt = sb("rt", [P, TT])
        ry = sb("ry", [P, TT])
        mx = sb("mx", [P, 2])
        nmx = sb("nmx", [P, 2, 2])
        psums = sb("psums", [P, 2, 2])
        rsum = sb("rsum", [P, 2])
        rtall = sb("rtall", [P, TT])
        gz, th, uz = yw[:, 0:2, :], yw[:, 2:4, :], yw[:, 4:6, :]
        zq, zk, shuf = yw[:, 0:2, :], yw[:, 2:4, :], yw[:, 4:6, :]
        pm = yw[:, 6:8, :]
        convb = hid[:, 18:20, :]
        att = hid[:, 16:18, :]
        cu = hid[:, 20:22, :]
        gatez = hid[:, 16:18, :]
        gateth = hid[:, 18:20, :]
        lamv = hid[:, 0, 0:DEPTH * 4 * HD]
        PS = ctx.enter_context(nc.psum_tensor("PS", [P, 8, T], f32))
        SC, TR, OB = 4, 6, 7

        nw_in, small_in, tables_in, y_out = sem("nw_in"), sem("small_in"), sem("tables_in"), sem("y_out")
        x_in = [sem(f"x_in{k}") for k in range(KT)]
        cleared, params = sem("cleared"), sem("params")
        lam_exp = sem("lam_exp")
        w_loaded = [sem("w_loaded0"), sem("w_loaded1")]
        w_hi, w_lo, w_used = sem("w_hi"), sem("w_lo"), sem("w_used")
        u_ready = sem("u_ready")
        x_new = [sem("x_even"), sem("x_odd")]
        x_hi, xw_ready = sem("x_hi"), sem("xw_ready")
        sq_ready, acc_done, acc_ready = sem("sq_ready"), sem("acc_done"), sem("acc_ready")
        stat, rt_ready, wide, r_ready = sem("stat"), sem("rt_ready"), sem("wide"), sem("r_ready")
        wide_read = sem("wide_read")
        gz_ready, th_ready, h_ready = sem("gz_ready"), sem("th_ready"), sem("h_ready")
        y_ready = sem("y_ready")
        y_scaled, co_read, ao_read = sem("y_scaled"), sem("co_read"), sem("ao_read")
        z_ready, q_hi, k_hi, qk_lo = sem("z_ready"), sem("q_hi"), sem("k_hi"), sem("qk_lo")
        v_hi, v_lo = sem("v_hi"), sem("v_lo")
        s_ready, s_max, s_exp = sem("s_ready"), sem("s_max"), sem("s_exp")
        a_ready = sem("a_ready")
        a_tr, a_hi, a_lo = sem("a_tr"), sem("a_hi"), sem("a_lo")
        pv, o_sq, o_stat, o_rt, o_wide, o_done = (sem("pv"), sem("o_sq"), sem("o_stat"), sem("o_rt"),
                                                    sem("o_wide"), sem("o_done"))
        cu_ready, conv_done = sem("cu_ready"), sem("conv_done")
        gate_z, gate_th, m_ready = sem("gate_z"), sem("gate_th"), sem("m_ready")

        block = ctx.enter_context(nc.Block())

        @block.sync
        def _(sp):
            def load(L, s, slot, src):
                sp.wait_ge(w_lo, L * STAGES + s + (RAW_CREDIT - 1))
                sp.dma_start(raw[:, slot, :].rearrange("p (k c) -> p k c", c=src.shape[-1]), src) \
                    .then_inc(w_loaded[slot], 16)

            def wide_src(w, L, col):
                return w[L, :, ds(col, 256)].rearrange("(k p) c -> p k c", p=P)

            def deep_src(w, L, row):
                return w[L, ds(row, 2 * P), :].rearrange("(k p) c -> p k c", p=P)

            def ffn(L, s0, w13, w2):
                a = s0 % 2
                with sp.Fori(0, UP) as i:
                    load(L, s0 + i * 2, a, wide_src(w13, L, i * 256))
                    load(L, s0 + i * 2 + 1, 1 - a, wide_src(w13, L, i * 256 + DFF))
                s1 = s0 + 2 * UP
                with sp.Fori(0, UP // 2) as i:
                    load(L, s1 + i * 2, a, deep_src(w2, L, i * 4 * P))
                    load(L, s1 + i * 2 + 1, 1 - a, deep_src(w2, L, i * 4 * P + 2 * P))
                load(L, s1 + UP - 1, a, deep_src(w2, L, (UP - 1) * 2 * P))

            def four(L, s0, src):
                for n in range(4):
                    load(L, s0 + n, (s0 + n) % 2, src(n))

            with sp.Fori(0, DEPTH) as L:
                ffn(L, 0, ffn1_w13, ffn1_w2)
                with sp.Fori(0, PAIRS) as i:
                    for n, first in enumerate((3 * D, 4 * D, 5 * D, 0, D, 2 * D)):
                        load(L, M0 + i * ATT + n, (M0 + n) % 2, wide_src(w_in, L, i * 256 + first))
                four(L, GC0, lambda n: wide_src(w_in, L, 6 * D + n * 256))
                four(L, CO0, lambda n: deep_src(w_conv_out, L, n * 2 * P))
                four(L, AO0, lambda n: deep_src(w_attn_out, L, n * 2 * P))
                four(L, GA0, lambda n: wide_src(w_in, L, 7 * D + n * 256))
                four(L, WO0, lambda n: deep_src(w_o, L, n * 2 * P))
                ffn(L, F20, ffn2_w13, ffn2_w2)
            for k in range(KT):
                sp.wait_ge(x_new[k % 2], DEPTH * (3 * KT // 2) + k // 2 + 1)
                sp.dma_start(out[k * P:(k + 1) * P, :], x[:, k, :]).then_inc(y_out, 16)
            sp.wait_ge(y_out, 16 * KT)

        @block.gpsimd
        def _(pool):
            pool.memset(ones[:, :], 1.0).then_inc(cleared, 1)
            pool.sem_inc(conv_done, CREDIT)
            pool.memset(ql[:, :, :].bitcast(f32), 0.0).then_inc(cleared, 1)
            for dst, src in ((bg, b_gateT), (cw, conv_wT), (sub, sublnT), (lamc, lam_const)):
                flat = dst[:, :] if len(dst.shape) == 2 else dst[:].rearrange(
                    "p a b -> p (a b)" if len(dst.shape) == 3 else "p a b c -> p (a b c)")
                pool.dma_start(flat, src[:, :]).then_inc(small_in, 16)
            for dst, src in ((ident, ident_in), (cosT, ropeC), (sinT, ropeS)):
                pool.dma_start(dst[:, :], src[:, :]).then_inc(tables_in, 16)

            def split(L, s, slot, after=False):
                if after:
                    pool.wait_ge(w_lo, L * STAGES + s + RAW_CREDIT)
                pool.wait_ge(w_hi, L * STAGES + s + 1)
                pool.tensor_tensor(wl[:, slot, :], raw[:, slot, :], wh[:, slot, :].bitcast(f32), ALU.subtract) \
                    .then_inc(w_lo, 1)

            def update(L, n, k, order=range(KT)):
                pool.wait_ge(u_ready, L * (3 * KT) + n * KT + order.index(k) + 1)
                pool.wait_ge(x_in[k], 16)
                pool.tensor_tensor(x[:, k, :], x[:, k, :], yw[:, k, :], ALU.add).then_inc(x_new[1], 1)

            def add(L, n, k, src):
                pool.wait_ge(sq_ready, L * (6 * KT) + n * KT + k + 1)
                if k > 1:
                    pool.wait_ge(acc_done, L * (6 * POOL_SUMS) + n * POOL_SUMS + k - 1)
                pool.tensor_tensor(acc[:, :], acc[:, :], src, ALU.add).then_inc(acc_done, 1)

            def pre(L, n):
                for step in (1, 3, -1, 5, -2, -3, 7, -4, -5):
                    if step > 0:
                        update(L, n, step)
                    else:
                        add(L, 2 * n, -step, yw[:, -step, :])

            def post(L, n):
                for k in range(1, POOL_SUMS + 1):
                    add(L, 2 * n + 1, k, sq[:, k % 2, :])

            with pool.Fori(0, DEPTH) as L:
                split(L, 0, 0, after=True)
                pre(L, 0)
                split(L, 2, 0)
                post(L, 0)
                split(L, M0 + 1, (M0 + 1) % 2, after=True)
                pre(L, 1)
                for n in range(3):
                    split(L, M0 + 2 + n, (M0 + n) % 2)

                def conv(i):
                    yc2 = hid[:, ds(i * 2, 2), :]

                    def tap(n):
                        for hh in range(2):
                            w3 = cw[:, ds(L, 1), n, ds(i * 2 + hh, 1)]
                            u = cu[:, hh:hh + 1, :]
                            yc = hid[:, ds(i * 2 + hh, 1), :]
                            if n == 1:
                                pool.tensor_tensor(yc, u, w3.to_broadcast([P, 1, T]), ALU.mult)
                                continue
                            to, of = (slice(1, T), slice(0, T - 1)) if n == 0 else (slice(0, T - 1), slice(1, T))
                            pool.tensor_tensor(sq[:, 0:1, to], u[:, :, of], w3.to_broadcast([P, 1, T - 1]), ALU.mult)
                            pool.drain()
                            pool.tensor_tensor(yc[:, :, to], yc[:, :, to], sq[:, 0:1, to], ALU.add)
                            pool.drain()
                        pool.drain()

                    def centre():
                        pool.wait_ge(cu_ready, L * PAIRS + i + 1)
                        pool.tensor_tensor(cu, cu, yc2, ALU.mult)
                        pool.drain()
                        tap(1)

                    def gate():
                        pool.tensor_tensor(yc2, yc2, convb, ALU.mult).then_inc(conv_done, 1)
                        pool.drain()
                    return centre, lambda: tap(0), lambda: tap(2), gate

                def beside(i, last):
                    for n in range(3):
                        split(L, M0 + 5 + i * ATT + n, (M0 + 1 + n) % 2)
                    for n, part in enumerate(conv(i)):
                        part()
                        if n == 0 or (not last and n < 3):
                            split(L, M0 + 8 + i * ATT + n, (M0 + n) % 2)

                with pool.Fori(0, PAIRS - 1) as i:
                    beside(i, False)
                beside(PAIRS - 1, True)
                post(L, 1)
                split(L, F20 + 1, (F20 + 1) % 2, after=True)
                pre(L, 2)
                split(L, F20 + 2, F20 % 2)
                post(L, 2)
            for k in range(1, KT, 2):
                update(DEPTH, 0, k, LAST_ORDER)

        @block.scalar
        def _(act):
            for credited in (s_exp, gate_th, y_scaled):
                act.sem_inc(credited, CREDIT)
            act.dma_start(nw[:, :, :, :].rearrange("p a b c -> p (a b c)"), norm_wT[:, :]).then_inc(nw_in, 16)
            act.dma_start(lamv, lam_vec.rearrange("l a d -> (l a d)").partition_broadcast(P)).then_inc(nw_in, 16)
            for k in range(KT):
                act.dma_start(x[:, k, :], xT[k * P:(k + 1) * P, :]).then_inc(x_in[k], 16)
            act.wait_ge(cleared, 1)
            act.activation(nmx[:, 0, :], ones[:, 0:2], ACT.Copy)

            def split(L, s, slot, src=None, ready=(), first=False):
                act.wait_ge(w_loaded[slot], L * (8 * STAGES) + s * 8 + (16 - 8 * slot))
                if not first:
                    act.wait_ge(w_used, L * STAGES + s - 1)
                for q, v in ready:
                    act.wait_ge(q, v)
                if src is not None:
                    act.activation(jit[:, slot, 0, :, :], src, ACT.Copy)
                act.activation(wh[:, slot, :], raw[:, slot, :], ACT.Copy).then_inc(w_hi, 1)

            def square(k, src, dst):
                act.activation(acc[:, :] if k == 0 else dst, src, ACT.Square).then_inc(sq_ready, 1)

            def pre(L, n):
                for k in range(KT):
                    act.wait_ge(x_new[k % 2], L * (3 * KT // 2) + n * KT // 2 + k // 2 + 1)
                    act.activation(xh[:, k, :], x[:, k, :], ACT.Copy, scale=nw[:, ds(L, 1), 2 * n, k]).then_inc(x_hi, 1)
                    square(k, x[:, k, :], yw[:, k, :])

            def rms(L, n):
                act.wait_ge(wide, L * 6 + 2 * n + 1 + CREDIT)
                act.activation(rpre[:, :], PS[:, 5, :], ACT.Copy).then_inc(r_ready, 1)

            def post(L, n):
                y0 = (0, 3 * KT, 4 * KT)[n]
                for m in range(KT):
                    act.wait_ge(y_ready, L * (5 * KT) + y0 + m + 1)
                    if m >= 3:
                        act.wait_ge(acc_done, L * (6 * POOL_SUMS) + (2 * n + 1) * POOL_SUMS + m - 2)
                    square(m, PS[:, m, :], sq[:, m % 2, :])
                    act.activation(yw[:, m, :], PS[:, m, :], ACT.Copy, scale=nw[:, ds(L, 1), 2 * n + 1, m]) \
                       .then_inc(y_scaled, 1)

            def ffn(L, w, s0, n):
                a = s0 % 2
                G = (L * 2 + w) * UP
                pre(L, n)

                def step(i, s, last, first=False):
                    def up_src(ii):
                        return hid[:, ds(ii * 2, 2), :]
                    split(L, s + 2, a, None if not last else up_src(0), [(h_ready, G + 1)] if last else ())
                    if first:
                        rms(L, n)
                    act.wait_ge(gz_ready, G + i + 1)
                    act.activation(th, gz, ACT.Tanh, scale=0.5).then_inc(th_ready, 1)
                    split(L, s + 3, 1 - a, None if not last else up_src(1), [(h_ready, G + 2)] if last else ())

                step(0, s0, False, first=True)
                with act.Fori(1, UP - 1) as i:
                    step(i, s0 + i * 2, False)
                step(UP - 1, s0 + 2 * (UP - 1), True)
                s1 = s0 + 2 * UP
                with act.Fori(0, (UP - 3) // 2) as i:
                    split(L, s1 + i * 2 + 2, a, hid[:, ds(i * 4 + 4, 2), :], [(h_ready, G + i * 2 + 3)])
                    split(L, s1 + i * 2 + 3, 1 - a, hid[:, ds(i * 4 + 6, 2), :], [(h_ready, G + i * 2 + 4)])
                split(L, s1 + UP - 1, a, hid[:, FT - 2:FT, :], [(h_ready, G + UP)])

            with act.Fori(0, DEPTH) as L:
                split(L, 0, 0, first=True)
                split(L, 1, 1, first=True)
                act.wait_ge(params, 1)
                ffn(L, 0, 0, 0)
                split(L, M0, 1)
                post(L, 0)
                split(L, M0 + 1, 0)
                pre(L, 1)
                act.activation(lexp[:, :], lsum[:, :], ACT.Exp).then_inc(lam_exp, 1)

                def qk(A, hh):
                    act.wait_ge(z_ready, A * 2 + 1 + hh)
                    if hh:
                        act.wait_ge(s_ready, A * 8 + 4)
                    for c in range(2):
                        for half in (c, 1 - c):
                            ins = act.activation(qhh[ROWS[half], c, :], zq[ROWS[c], hh, :], ACT.Copy)
                    ins.then_inc(q_hi, 1)
                    act.wait_ge(z_ready, A * 2 + 2)
                    for c in range(2):
                        ins = act.activation(khl[ROWS[c], c, :], zk[ROWS[c], hh, :], ACT.Copy)
                    ins.then_inc(k_hi, 1)

                def softmax(A, j):
                    act.wait_ge(s_max, A * 8 + j + 1)
                    for c in range(2):
                        act.activation(pm[:, c, :], PS[:, SC + c, :], ACT.Exp, bias=nmx[:, j % 2, c:c + 1], scale=SCALE,
                                       accum_out=psums[:, j % 2, c:c + 1]).then_inc(s_exp, 1)

                def a_evac(A, j):
                    act.wait_ge(a_tr, A * 8 + j + 1)
                    if j % 4 == 0:
                        act.wait_ge(pv, A * 2 + j // 4 + CREDIT)
                    act.activation(aT[:, 0, :, (j % 4) * P:(j % 4 + 1) * P],
                                   PS[:, TR, :].rearrange("p (k q) -> p k q", q=P), ACT.Copy).then_inc(a_hi, 1)

                def v_split(i, s):
                    act.wait_ge(w_used, L * STAGES + s + 1)
                    for t in range(TT):
                        ins = act.activation(vh[:, t, :, :], PS[:, t // 2, (t % 2) * 256:(t % 2 + 1) * 256]
                                             .rearrange("p (h d) -> p h d", d=P), ACT.Copy, scale=rtall[:, t:t + 1])
                    ins.then_inc(v_hi, 1)

                def o_evac(A, i, hh):
                    act.wait_ge(pv, A * 2 + hh + 1 + CREDIT)
                    act.activation(sq[:, 1, :], PS[:, OB, :], ACT.Square)
                    act.activation(hid[:, ds(i * 2 + 8 + hh, 1), :], PS[:, OB, :].unsqueeze(1), ACT.Copy).then_inc(o_sq, 1)

                def attend(i):
                    A = L * PAIRS + i
                    s = M0 + i * ATT + 3
                    softmax(A, 0)
                    softmax(A, 1)
                    a_evac(A, 0)
                    softmax(A, 2)
                    split(L, s + 2, (M0 + 3) % 2)
                    a_evac(A, 1)
                    softmax(A, 3)
                    qk(A, 1)
                    a_evac(A, 2)
                    softmax(A, 4)
                    split(L, s + 3, M0 % 2)
                    a_evac(A, 3)
                    softmax(A, 5)
                    o_evac(A, i, 0)
                    a_evac(A, 4)
                    softmax(A, 6)
                    split(L, s + 4, (M0 + 1) % 2)
                    a_evac(A, 5)
                    softmax(A, 7)
                    a_evac(A, 6)
                    split(L, s + 5, M0 % 2)
                    a_evac(A, 7)
                    o_evac(A, i, 1)

                split(L, M0 + 2, M0 % 2)
                rms(L, 1)
                act.wait_ge(cleared, 2)
                split(L, M0 + 3, (M0 + 1) % 2)
                qk(L * PAIRS, 0)
                v_split(0, M0 + 2)
                split(L, M0 + 4, M0 % 2)
                with act.Fori(0, PAIRS - 1) as i:
                    attend(i)
                    s = M0 + i * ATT + ATT
                    split(L, s + 3, (M0 + 1) % 2)
                    qk(L * PAIRS + i + 1, 0)
                    v_split(i + 1, s + 2)
                    split(L, s + 4, M0 % 2)
                attend(PAIRS - 1)

                def gate(n, g, t, dst):
                    act.wait_ge(gate_z, L * 8 + 4 * g + t + 1)
                    for j in range(2):
                        ins = act.activation(dst[:, j, :], gatez[:, j, :], ACT.Tanh, scale=0.5,
                                             bias=bgh[:, ds(L, 1), g, 2 * t + j])
                    ins.then_inc(gate_th, 1)

                for t in range(4):
                    if t == 1:
                        split(L, GC0 + t + 2, (GC0 + t) % 2)
                    elif t > 1:
                        split(L, GC0 + t + 2, (GC0 + t) % 2, hid[:, 2 * t - 4:2 * t - 2, :], [(conv_done, L * PAIRS + t - 1 + CREDIT)])
                    gate(GC0, 0, t, yw[:, 2 * t:2 * t + 2, :])
                for t in range(4):
                    if t < 2:
                        split(L, CO0 + t + 2, (CO0 + t) % 2, hid[:, 2 * t + 4:2 * t + 6, :], [(conv_done, L * PAIRS + t + 3 + CREDIT)])
                    else:
                        split(L, CO0 + t + 2, (CO0 + t) % 2, hid[:, 2 * t + 4:2 * t + 6, :], [(o_done, L * HEADS + 2 * t - 2 + CREDIT)])
                for t in range(2):
                    split(L, AO0 + t + 2, (AO0 + t) % 2, hid[:, 2 * t + 12:2 * t + 14, :], [(o_done, L * HEADS + 2 * t + 6 + CREDIT)])
                split(L, AO0 + 4, AO0 % 2)
                for m in range(KT):
                    act.wait_ge(y_ready, L * (5 * KT) + 2 * KT + m + 1)
                    act.activation(hid[:, 8 + m, :], PS[:, m, :], ACT.Copy, scale=0.5).then_inc(ao_read, 1)
                split(L, AO0 + 5, (AO0 + 1) % 2)
                for t in range(4):
                    if t < 2:
                        split(L, GA0 + t + 2, (GA0 + t) % 2)
                    else:
                        split(L, GA0 + t + 2, (GA0 + t) % 2, hid[:, 2 * t - 4:2 * t - 2, :], [(m_ready, L * 4 + t - 1)])
                    gate(GA0, 1, t, gateth)
                for t in range(3):
                    if t < 2:
                        split(L, WO0 + t + 2, (WO0 + t) % 2, hid[:, 2 * t + 4:2 * t + 6, :], [(m_ready, L * 4 + t + 3)])
                    else:
                        split(L, F20, F20 % 2)
                post(L, 1)
                split(L, F20 + 1, (F20 + 1) % 2)
                ffn(L, 1, F20, 2)
                post(L, 2)

        @block.tensor
        def _(pe):
            for credited in (pv, wide):
                pe.sem_inc(credited, CREDIT)
            pe.wait_ge(cleared, 2)

            def product(bank, slot, off, xhi, xlo, start, stop):
                hi, lo = wh[:, slot, off:off + P], wl[:, slot, off:off + P]
                pe.matmul(PS[:, bank, :], hi, xhi, start=start, stop=False)
                pe.matmul(PS[:, bank, :], hi, xlo, start=False, stop=False)
                return pe.matmul(PS[:, bank, :], lo, xhi, start=False, stop=stop)

            def wide_parts(L, s, slot, ordinal, banks, norm=None):
                def go(w, xx, k, j, wait=None, start=False, stop=False, used=False):
                    def run():
                        if wait:
                            wait()
                        mm = pe.matmul(PS[:, banks + j, :], w[:, slot, k * 256 + j * P:k * 256 + (j + 1) * P], xx[:, k, :],
                                       start=start, stop=stop)
                        if used:
                            mm.then_inc(w_used, 1)
                    return run

                def begin():
                    pe.wait_ge(w_hi, L * STAGES + s + 1)
                    pe.wait_ge(wide_read, L * WIDE + ordinal + (READ_CREDIT - 1))
                    input_hi(0)

                def input_hi(k):
                    if norm is not None:
                        pe.wait_ge(x_hi, L * (3 * KT) + norm * KT + k + 1)

                def input_lo(k):
                    if norm is not None:
                        pe.wait_ge(xw_ready, L * (3 * KT) + norm * KT + k + 1)

                def weights_lo():
                    pe.wait_ge(w_lo, L * STAGES + s + (RAW_CREDIT + 1))

                hi = [[go(wh, xh, k, 0, begin if k == 0 else lambda k=k: input_hi(k), start=(k == 0)),
                       go(wh, xh, k, 1, start=(k == 0)),
                       go(wh, xl, k, 0, lambda k=k: input_lo(k)),
                       go(wh, xl, k, 1)] for k in range(KT)]
                lo = [go(wl, xh, k, j, weights_lo if (k, j) == (0, 0) else None, stop=(k == KT - 1),
                         used=(k, j) == (KT - 1, 1)) for k in range(KT) for j in range(2)]
                return hi, lo

            def wide_ops(*a, **kw):
                hi, lo = wide_parts(*a, **kw)
                passes = [p for tile in hi for p in tile] + lo

                def step(three):
                    def run():
                        for p in three:
                            p()
                    return run
                return [step(passes[n:n + 3]) for n in range(0, len(passes), 3)]

            def wide_stage(*a, **kw):
                for op in wide_ops(*a, **kw):
                    op()

            def norm_stat(L, n, eighth=None):
                pe.wait_ge(acc_ready, L * 6 + n + 1)
                for t in range(TT):
                    mm = pe.matmul(PS[:, 4, t:t + 1], acc[:, t * P:(t + 1) * P], ones[:, 0:1], start=(t == 0),
                                   stop=(eighth is None and t == TT - 1), skip_group_check=True)
                if eighth is not None:
                    pe.wait_ge(sq_ready, L * (6 * KT) + n * KT + KT)
                    for t in range(TT):
                        mm = pe.matmul(PS[:, 4, t:t + 1], eighth[:, t * P:(t + 1) * P], ones[:, 0:1], start=False,
                                       stop=(t == TT - 1), skip_group_check=True)
                mm.then_inc(stat, 1)

            def spread(bank, done):
                for t in range(TT):
                    mm = pe.transpose(PS[:, bank, t * P:(t + 1) * P], ry[:, t:t + 1].to_broadcast([P, P]), ident[:, :])
                mm.then_inc(done, 1)

            def norm_wide(L, n):
                pe.wait_ge(rt_ready, L * 6 + n + 1)
                pe.wait_ge(tables_in, 16 * 3)
                spread(5, wide)

            def first_pair(L, s, ordinal, n):
                (a, a_lo), (b, b_lo) = (wide_parts(L, s + q, (s + q) % 2, ordinal + q, 2 * q, norm=n) for q in range(2))
                for k in range(KT):
                    for p in a[k] + b[k]:
                        p()
                rest = a_lo + b_lo
                for p in rest[:6]:
                    p()
                norm_stat(L, 2 * n)
                for p in rest[6:20]:
                    p()
                norm_wide(L, 2 * n)
                for p in rest[20:]:
                    p()

            def deep_stage(L, s, slot, first, last, bank_free=None, order=(4, 5, 6, 7, 0, 1, 2, 3)):
                pe.wait_ge(w_lo, L * STAGES + s + (RAW_CREDIT + 1))
                for m in (order if first else range(KT)):
                    if bank_free is not None:
                        bank_free(m)
                    for kk in range(2):
                        mm = product(m, slot, kk * D + m * P, jit[:, slot, 0, kk, :], jit[:, slot, 1, kk, :],
                                     first and kk == 0, last and kk == 1)
                    if last:
                        mm.then_inc(y_ready, 1)
                if last:
                    pe.drain()
                    pe.sem_inc(w_used, 1)
                else:
                    mm.then_inc(w_used, 1)

            def ffn(L, s0, ordinal, n):
                a = s0 % 2
                first_pair(L, s0, ordinal, n)
                with pe.Fori(1, UP) as i:
                    wide_stage(L, s0 + i * 2, a, ordinal + i * 2, 0)
                    wide_stage(L, s0 + i * 2 + 1, 1 - a, ordinal + i * 2 + 1, 2)
                s1 = s0 + 2 * UP

                def free(m):
                    if m == 0:
                        pe.wait_ge(wide_read, L * WIDE + ordinal + 2 * UP + READ_CREDIT)
                deep_stage(L, s1, a, True, False, free)
                with pe.Fori(0, (UP - 3) // 2) as i:
                    deep_stage(L, s1 + i * 2 + 1, 1 - a, False, False)
                    deep_stage(L, s1 + i * 2 + 2, a, False, False)
                deep_stage(L, s1 + UP - 2, 1 - a, False, False)
                deep_stage(L, s1 + UP - 1, a, False, True)
                norm_stat(L, 2 * n + 1, sq[:, 1, :])
                norm_wide(L, 2 * n + 1)

            with pe.Fori(0, DEPTH) as L:
                ffn(L, 0, 0, 0)
                o0 = 2 * UP
                o1 = o0 + ATT * PAIRS
                first_pair(L, M0, o0, 1)

                def v_ops(L, s, slot, ordinal):
                    def go(t, k, xx, w, wait=None, start=False, stop=False, used=False):
                        def run():
                            if wait:
                                wait()
                            mm = pe.matmul(PS[:, t // 2, (t % 2) * 256:(t % 2 + 1) * 256], xx[:, k, t * P:(t + 1) * P],
                                           w[:, slot, k * 256:(k + 1) * 256], start=start, stop=stop, skip_group_check=True)
                            if used:
                                mm.then_inc(w_used, 1)
                        return run

                    def begin():
                        pe.wait_ge(w_hi, L * STAGES + s + 1)
                        pe.wait_ge(wide_read, L * WIDE + ordinal + (READ_CREDIT - 1))

                    def weights_lo():
                        pe.wait_ge(w_lo, L * STAGES + s + (RAW_CREDIT + 1))

                    passes = [go(t, k, xx, wh, begin if (t, k) == (0, 0) and xx is xh else None,
                                 start=(k == 0 and t % 2 == 0 and xx is xh))
                              for t in range(TT) for k in range(KT) for xx in (xh, xl)]
                    passes += [go(t, k, xh, wl, weights_lo if (t, k) == (0, 0) else None, stop=(k == KT - 1),
                                  used=(t, k) == (TT - 1, KT - 1)) for t in range(TT) for k in range(KT)]

                    def step(six):
                        def run():
                            for p in six:
                                p()
                        return run
                    return [step(passes[n:n + 6]) for n in range(0, len(passes), 6)]

                def stage_ops(i, n):
                    s, slot, o = M0 + i * ATT + n, (M0 + n) % 2, o0 + i * ATT + n
                    return v_ops(L, s, slot, o) if n == 2 else wide_ops(L, s, slot, o, 2 * (n % 2))

                def work(flow, n):
                    for _ in range(n):
                        flow.pop(0)()

                def scores(A, j):
                    hh, qt = j // 4, j % 4
                    if qt == 0:
                        pe.wait_ge(qk_lo, A * 2 + hh + 1)
                    pe.wait_ge(s_exp, A * 16 + 2 * j + CREDIT)
                    q = slice(qt * P, (qt + 1) * P)
                    for c in range(2):
                        pe.matmul(PS[:, SC + c, :], qhh[:, c, q], khl[:, c, :], start=True, stop=False)
                        mm = pe.matmul(PS[:, SC + c, :], ql[:, c, q], khl[:, c, :], start=False, stop=True)
                    mm.then_inc(s_ready, 1)

                def a_transpose(A, j):
                    pe.wait_ge(a_ready, A * 8 + j + 1)
                    pe.wait_ge(a_lo, A * 8 + j + CREDIT)
                    for kt in range(TT):
                        mm = pe.transpose(PS[:, TR, kt * P:(kt + 1) * P], att[:, j % 2, kt * P:(kt + 1) * P], ident[:, :])
                    mm.then_inc(a_tr, 1)

                def values(A, hh):
                    pe.wait_ge(a_lo, A * 8 + 4 * hh + 4 + CREDIT)
                    pe.wait_ge(v_lo, A + 1)
                    pe.wait_ge(o_done, A * 2 + hh + CREDIT)
                    for kt in range(TT):
                        pe.matmul(PS[:, OB, :], vh[:, kt, hh, :], aT[:, 0, kt, :], start=(kt == 0), stop=False)
                        pe.matmul(PS[:, OB, :], vh[:, kt, hh, :], aT[:, 1, kt, :], start=False, stop=False)
                        mm = pe.matmul(PS[:, OB, :], vl[:, kt, hh, :], aT[:, 0, kt, :], start=False, stop=(kt == TT - 1))
                    mm.then_inc(pv, 1)

                def out_stat(A, hh):
                    pe.wait_ge(o_sq, A * 2 + hh + 1)
                    for t in range(TT):
                        mm = pe.matmul(PS[:, OB, t:t + 1], sq[:, 1, t * P:(t + 1) * P], ones[:, 0:1], start=True, stop=True)
                    mm.then_inc(o_stat, 1)

                def out_wide(A, hh):
                    pe.wait_ge(o_rt, A * 2 + hh + 1)
                    spread(OB, o_wide)

                def attend(i, following):
                    A = L * PAIRS + i
                    flow = stage_ops(i, 3) + stage_ops(i, 4) + stage_ops(i, 5) + following
                    work(flow, 5)
                    for j, steps in enumerate((6, 6, 6, 12, 6, 6, 6, 8)):
                        scores(A, j)
                        work(flow, steps)
                        if j == 5:
                            values(A, 0)
                        if j == 6:
                            out_stat(A, 0)
                        if j == 7:
                            out_wide(A, 0)
                        if j:
                            a_transpose(A, j - 1)
                    work(flow, 5)
                    a_transpose(A, 7)
                    work(flow, 5)
                    values(A, 1)
                    work(flow, 3)
                    out_stat(A, 1)
                    work(flow, 5)
                    out_wide(A, 1)
                    work(flow, len(flow))

                work(v := stage_ops(0, 2), len(v))
                with pe.Fori(0, PAIRS - 1) as i:
                    attend(i, stage_ops(i + 1, 0) + stage_ops(i + 1, 1) + stage_ops(i + 1, 2))
                attend(PAIRS - 1, [op for t in range(4) for op in
                                   wide_ops(L, GC0 + t, (GC0 + t) % 2, o1 + t, 2 * (t % 2))])
                for t in range(4):
                    def gates_read(m):
                        if m == 0:
                            pe.wait_ge(wide_read, L * WIDE + o1 + 4 + READ_CREDIT)
                        if m == 4:
                            pe.wait_ge(o_done, L * HEADS + HEADS + CREDIT)
                    deep_stage(L, CO0 + t, (CO0 + t) % 2, t == 0, t == 3, gates_read if t == 0 else None)
                for t in range(4):
                    def conv_read(m):
                        pe.wait_ge(co_read, L * KT + m + 1)
                    deep_stage(L, AO0 + t, (AO0 + t) % 2, t == 0, t == 3, conv_read if t == 0 else None, range(KT))
                for t in range(4):
                    pe.wait_ge(ao_read, L * KT + min(2 * t + 2, 4))
                    wide_stage(L, GA0 + t, (GA0 + t) % 2, o1 + 4 + t, 2 * (t % 2))
                for t in range(4):
                    def gates_read2(m):
                        if m == 4:
                            pe.wait_ge(ao_read, L * KT + KT)
                        if m == 0:
                            pe.wait_ge(wide_read, L * WIDE + o1 + 8 + READ_CREDIT)
                    deep_stage(L, WO0 + t, (WO0 + t) % 2, t == 0, t == 3, gates_read2 if t == 0 else None)
                norm_stat(L, 3, sq[:, 1, :])
                norm_wide(L, 3)
                ffn(L, F20, o1 + 8, 2)

        @block.vector
        def _(dve):
            for _ in range(RAW_CREDIT):
                dve.memset(rv[:, :], 0.0).then_inc(w_lo, 1)
                dve.drain()
            for credited in (a_lo, o_done):
                dve.sem_inc(credited, CREDIT)
            for _ in range(READ_CREDIT):
                dve.drain()
                dve.memset(rv[:, :], 0.0).then_inc(wide_read, 1)
            dve.memset(yw[:, :, :], 0.0)
            dve.memset(PS[:, 5, :], 0.0)
            dve.wait_ge(nw_in, 32)
            for n in (1, 5):
                dve.tensor_scalar(nw[:, :, n, :], nw[:, :, n, :], 0.5, None, ALU.mult)
            lv = lamv.rearrange("p (l a b d) -> p (l a) b d", l=DEPTH, a=2, b=2)
            prod = hid[:, 1, 0:DEPTH * 2 * HD].rearrange("p (l d) -> p l d", d=HD)
            dve.tensor_tensor(prod, lv[:, :, 0, :], lv[:, :, 1, :], ALU.mult)
            dve.drain()
            dve.tensor_reduce(lsum[:, :], prod, AX.X, ALU.add).then_inc(params, 1)

            def derive(L):
                dve.wait_ge(small_in, 16 * 4)
                dve.tensor_scalar(bgh[:, :, :, :], bg[:, :, :, :], 0.5, None, ALU.mult)
                dve.tensor_tensor(subs[:, :], sub[:, :], lamc[:, 1, :], ALU.mult)
                dve.wait_ge(lam_exp, L + 1)
                le = lexp[:, :].rearrange("p (l a) -> p l a", a=2)
                dve.tensor_tensor(nlam[:, :], le[:, :, 1], le[:, :, 0], ALU.subtract)
                dve.drain()
                dve.tensor_tensor(nlam[:, :], nlam[:, :], lamc[:, 0, :], ALU.subtract)
                dve.drain()

            def rsqrt(bank_cols, count, done):
                c = math.sqrt(0.375)
                dve.tensor_scalar(rv[:, :], bank_cols, 1.0 / count, EPS, ALU.mult, ALU.add)
                dve.drain()
                dve.tensor_scalar(rt[:, :].bitcast(i32), rv[:, :].bitcast(i32), 1, None, ALU.logical_shift_right)
                dve.tensor_scalar(rw[:, :], rv[:, :], c, None, ALU.mult)
                dve.drain()
                dve.tensor_scalar(ry[:, :].bitcast(i32), rt[:, :].bitcast(i32), -1.0, float(0x5F3759DF), ALU.mult, ALU.add)
                dve.drain()
                dve.tensor_tensor(rt[:, :], ry[:, :], ry[:, :], ALU.mult)
                dve.drain()
                dve.tensor_tensor(rt[:, :], rt[:, :], rw[:, :], ALU.mult)
                dve.drain()
                dve.scalar_tensor_tensor(out=rt[:, :], in0=rt[:, :], scalar=-1.25 / c, in1=rt[:, :], op0=ALU.add, op1=ALU.mult)
                dve.drain()
                dve.scalar_tensor_tensor(out=ry[:, :], in0=rt[:, :], scalar=1.875, in1=ry[:, :], op0=ALU.add, op1=ALU.mult)
                dve.drain()
                dve.tensor_tensor(rt[:, :], ry[:, :], ry[:, :], ALU.mult)
                dve.drain()
                dve.scalar_tensor_tensor(out=rt[:, :], in0=rt[:, :], scalar=-0.5, in1=rv[:, :], op0=ALU.mult, op1=ALU.mult)
                dve.drain()
                dve.scalar_tensor_tensor(out=ry[:, :], in0=rt[:, :], scalar=1.5, in1=ry[:, :], op0=ALU.add, op1=ALU.mult) \
                    .then_inc(done, 1)
                dve.drain()

            def split(L, s, slot, src=None, after=False):
                if after:
                    dve.wait_ge(w_lo, L * STAGES + s + RAW_CREDIT)
                dve.wait_ge(w_hi, L * STAGES + s + 1)
                if src is not None:
                    dve.tensor_tensor(jit[:, slot, 1, :, :], src, jit[:, slot, 0, :, :].bitcast(f32), ALU.subtract)
                dve.tensor_tensor(wl[:, slot, :], raw[:, slot, :], wh[:, slot, :].bitcast(f32), ALU.subtract).then_inc(w_lo, 1)

            def x_lo(L, n, k):
                dve.wait_ge(x_hi, L * (3 * KT) + n * KT + k + 1)
                dve.scalar_tensor_tensor(out=xl[:, k, :], in0=x[:, k, :], scalar=nw[:, ds(L, 1), 2 * n, k],
                                         in1=xh[:, k, :].bitcast(f32), op0=ALU.mult, op1=ALU.subtract).then_inc(xw_ready, 1)

            def norm(L, n, seventh, eighth=None):
                dve.wait_ge(acc_done, L * (6 * POOL_SUMS) + (n + 1) * POOL_SUMS)
                dve.wait_ge(sq_ready, L * (6 * KT) + n * KT + KT - 1)
                if eighth is None:
                    dve.tensor_tensor(acc[:, :], acc[:, :], seventh, ALU.add).then_inc(acc_ready, 1)
                else:
                    dve.tensor_tensor(acc[:, :], acc[:, :], seventh, ALU.add)
                    dve.drain()
                    dve.wait_ge(sq_ready, L * (6 * KT) + n * KT + KT)
                    dve.tensor_tensor(acc[:, :], acc[:, :], eighth, ALU.add).then_inc(acc_ready, 1)
                dve.wait_ge(stat, L * 6 + n + 1)
                rsqrt(PS[:, 4, 0:TT], D, rt_ready)

            def pre_norm(L, n):
                norm(L, 2 * n, yw[:, KT - 2, :], yw[:, KT - 1, :])

            def post_norm(L, n):
                norm(L, 2 * n + 1, sq[:, 0, :])

            def due(L, n, k):
                if k == 0:
                    dve.wait_ge(wide, L * 6 + 2 * n + CREDIT)
                    dve.wait_ge(y_scaled, L * (3 * KT) + n * KT + CREDIT)
                dve.tensor_tensor(yw[:, k, :], PS[:, 5, :], yw[:, k, :], ALU.mult).then_inc(u_ready, 1)

            def add(k):
                dve.wait_ge(x_in[k], 16)
                dve.tensor_tensor(x[:, k, :], x[:, k, :], yw[:, k, :], ALU.add).then_inc(x_new[k % 2], 1)

            def update(L, n, s=None):
                for k in range(KT):
                    due(L, n, k)
                    if k % 2 == 0:
                        dve.drain()
                        add(k)
                    else:
                        if k == KT - 1 and s is not None:
                            split(L, s, s % 2, after=True)
                    if k:
                        x_lo(L, n, k - 1)
                x_lo(L, n, KT - 1)

            def rows(t):
                return t.unsqueeze(1).to_broadcast([P, 2, T])

            def scaled(dst, bank, done):
                dve.tensor_tensor(dst, PS[:, bank:bank + 2, :], rows(rpre[:, :]), ALU.mult).then_inc(done, 1)

            def used(L, s):
                dve.wait_ge(w_used, L * STAGES + s + 1)

            def ffn(L, w, s0, n):
                a = s0 % 2
                G = (L * 2 + w) * UP
                pre_norm(L, n)

                def step(i, s, last, first=False):
                    used(L, s)
                    dve.wait_ge(r_ready, L * 3 + n + 1)
                    scaled(gz, 0, wide_read)
                    dve.drain()
                    dve.sem_inc(gz_ready, 1)
                    if not first:
                        split(L, s + 2, a, hid[:, 0:2, :] if last else None)
                    used(L, s + 1)
                    scaled(uz, 2, wide_read)
                    split(L, s + 3, 1 - a, hid[:, 2:4, :] if last else None, after=first)
                    dve.wait_ge(th_ready, G + i + 1)
                    dve.scalar_tensor_tensor(out=gz, in0=th, scalar=1.0, in1=gz, op0=ALU.add, op1=ALU.mult)
                    dve.drain()
                    dve.scalar_tensor_tensor(out=hid[:, ds(i * 2, 2), :], in0=gz, scalar=0.5, in1=uz,
                                             op0=ALU.mult, op1=ALU.mult).then_inc(h_ready, 1)
                    dve.drain()

                step(0, s0, False, first=True)
                with dve.Fori(1, UP - 1) as i:
                    step(i, s0 + i * 2, False)
                step(UP - 1, s0 + 2 * (UP - 1), True)
                s1 = s0 + 2 * UP
                with dve.Fori(0, (UP - 3) // 2) as i:
                    split(L, s1 + i * 2 + 2, a, hid[:, ds(i * 4 + 4, 2), :])
                    split(L, s1 + i * 2 + 3, 1 - a, hid[:, ds(i * 4 + 6, 2), :])
                split(L, s1 + UP - 1, a, hid[:, FT - 2:FT, :])

            with dve.Fori(0, DEPTH) as L:
                update(L, 0, 1)
                ffn(L, 0, 0, 0)
                split(L, M0, 1)
                post_norm(L, 0)
                update(L, 1)

                def rope(z, bank):
                    scaled(z, bank, wide_read)
                    dve.drain()
                    dve.stream_shuffle(shuf, z, list(range(8, 16)) + list(range(8)) + list(range(16, 32)))
                    dve.drain()
                    dve.tensor_tensor(shuf, shuf, rows(sinT[:, :]), ALU.mult)
                    dve.tensor_tensor(z, z, rows(cosT[:, :]), ALU.mult)
                    dve.drain()
                    dve.tensor_tensor(z, z, shuf, ALU.add).then_inc(z_ready, 1)
                    dve.drain()

                def q_lo(A, hh):
                    dve.wait_ge(q_hi, A * 2 + hh + 1)
                    for c in range(2):
                        dve.tensor_tensor(ql[ROWS[c], c, :], zq[ROWS[c], hh, :], qhh[ROWS[c], c, :].bitcast(f32),
                                          ALU.subtract)

                def k_lo(A, hh):
                    dve.wait_ge(k_hi, A * 2 + hh + 1)
                    for c in range(2):
                        ins = dve.tensor_tensor(khl[ROWS[1 - c], c, :], zk[ROWS[c], hh, :],
                                                khl[ROWS[c], c, :].bitcast(f32), ALU.subtract)
                    ins.then_inc(qk_lo, 1)

                def row_max(A, j):
                    dve.wait_ge(s_ready, A * 8 + j + 1)
                    dve.tensor_reduce(mx[:, :], PS[:, SC:SC + 2, :], AX.X, ALU.max)
                    dve.drain()
                    dve.tensor_scalar(nmx[:, j % 2, :], mx[:, :], -SCALE, None, ALU.mult).then_inc(s_max, 1)

                def combine(A, j):
                    dve.wait_ge(s_exp, A * 16 + 2 * j + 2 + CREDIT)
                    dve.reciprocal(rsum[:, :], psums[:, j % 2, :])
                    dve.drain()
                    if j >= 2:
                        dve.wait_ge(a_tr, A * 8 + j - 1)
                    dve.tensor_scalar(att[:, j % 2, :], pm[:, 1, :], rsum[:, 1:2], nlam[:, ds(L, 1)], ALU.mult, ALU.mult)
                    dve.drain()
                    dve.scalar_tensor_tensor(out=att[:, j % 2, :], in0=pm[:, 0, :], scalar=rsum[:, 0:1], in1=att[:, j % 2, :],
                                             op0=ALU.mult, op1=ALU.add).then_inc(a_ready, 1)

                def a_evac(A, j):
                    dve.wait_ge(a_hi, A * 8 + j + 1)
                    sl = slice((j % 4) * P, (j % 4 + 1) * P)
                    dve.tensor_tensor(aT[:, 1, :, sl], PS[:, TR, :].rearrange("p (k q) -> p k q", q=P),
                                      aT[:, 0, :, sl].bitcast(f32), ALU.subtract).then_inc(a_lo, 1)

                def v_split(A):
                    dve.wait_ge(v_hi, A + 1)
                    for t in range(TT):
                        ins = dve.scalar_tensor_tensor(
                            out=vl[:, t, :, :], in0=PS[:, t // 2, (t % 2) * 256:(t % 2 + 1) * 256].rearrange("p (h d) -> p h d", d=P),
                            scalar=rtall[:, t:t + 1], in1=vh[:, t, :, :].bitcast(f32), op0=ALU.mult, op1=ALU.subtract)
                    ins.then_inc(v_lo, 1)

                def out_norm(A, hh):
                    dve.wait_ge(o_stat, A * 2 + hh + 1)
                    rsqrt(PS[:, OB, 0:TT], P, o_rt)

                def out_scale(A, i, hh):
                    dve.wait_ge(o_wide, A * 2 + hh + 1)
                    o = hid[:, ds(i * 2 + 8 + hh, 1), :]
                    dve.scalar_tensor_tensor(out=o, in0=o, scalar=subs[:, ds(L, 1)], in1=PS[:, OB, :].unsqueeze(1),
                                             op0=ALU.mult, op1=ALU.mult).then_inc(o_done, 1)

                def q_rope(i):
                    used(L, M0 + i * ATT)
                    rope(zq, 0)

                def k_rope(i):
                    used(L, M0 + i * ATT + 1)
                    rope(zk, 2)
                    q_lo(L * PAIRS + i, 0)
                    k_lo(L * PAIRS + i, 0)

                def gate_logits(s, t, first_gate):
                    used(L, s + t)
                    if first_gate:
                        dve.wait_ge(gate_th, L * 8 + t + CREDIT)
                    scaled(gatez, 2 * (t % 2), wide_read)
                    dve.drain()
                    dve.sem_inc(gate_z, 1)

                def attend(i, following):
                    A, s = L * PAIRS + i, M0 + i * ATT + 3
                    row_max(A, 0)
                    v_split(A)
                    dve.drain()
                    dve.sem_inc(wide_read, 1)
                    combine(A, 0)
                    row_max(A, 1)
                    combine(A, 1)
                    row_max(A, 2)
                    a_evac(A, 0)
                    combine(A, 2)
                    used(L, s)
                    dve.wait_ge(conv_done, A + CREDIT)
                    scaled(convb, 2, wide_read)
                    row_max(A, 3)
                    a_evac(A, 1)
                    combine(A, 3)
                    q_lo(A, 1)
                    k_lo(A, 1)
                    row_max(A, 4)
                    a_evac(A, 2)
                    combine(A, 4)
                    used(L, s + 1)
                    scaled(hid[:, ds(i * 2, 2), :], 0, wide_read)
                    row_max(A, 5)
                    a_evac(A, 3)
                    combine(A, 5)
                    row_max(A, 6)
                    a_evac(A, 4)
                    combine(A, 6)
                    used(L, s + 2)
                    scaled(cu, 2, wide_read)
                    dve.drain()
                    dve.sem_inc(cu_ready, 1)
                    out_norm(A, 0)
                    row_max(A, 7)
                    a_evac(A, 5)
                    combine(A, 7)
                    out_scale(A, i, 0)
                    a_evac(A, 6)
                    a_evac(A, 7)
                    following()
                    out_norm(A, 1)
                    out_scale(A, i, 1)

                pre_norm(L, 1)
                dve.tensor_copy(rtall[:, :], ry[:, :])
                derive(L)
                dve.wait_ge(r_ready, L * 3 + 2)
                q_rope(0)
                k_rope(0)
                with dve.Fori(0, PAIRS - 1) as i:
                    attend(i, lambda: q_rope(i + 1))
                    k_rope(i + 1)
                attend(PAIRS - 1, lambda: gate_logits(GC0, 0, True))

                for t in range(4):
                    if t:
                        gate_logits(GC0, t, True)
                    if t == 1:
                        split(L, GC0 + t + 2, (GC0 + t) % 2, after=True)
                    elif t > 1:
                        split(L, GC0 + t + 2, (GC0 + t) % 2, hid[:, 2 * t - 4:2 * t - 2, :])
                for t in range(3):
                    split(L, CO0 + t + 2, (CO0 + t) % 2, hid[:, 2 * t + 4:2 * t + 6, :])
                dve.wait_ge(gate_th, L * 8 + 4 + CREDIT)
                for m in range(KT):
                    dve.wait_ge(y_ready, L * (5 * KT) + KT + m + 1)
                    dve.scalar_tensor_tensor(out=hid[:, m, :], in0=yw[:, m, :], scalar=1.0, in1=PS[:, m, :],
                                             op0=ALU.add, op1=ALU.mult).then_inc(co_read, 1)
                split(L, CO0 + 5, (CO0 + 3) % 2, hid[:, 10:12, :])
                for t in range(4):
                    if t < 2:
                        split(L, AO0 + t + 2, (AO0 + t) % 2, hid[:, 2 * t + 12:2 * t + 14, :])
                    else:
                        split(L, AO0 + t + 2, (AO0 + t) % 2)
                dve.wait_ge(ao_read, L * KT + KT)
                for t in range(4):
                    gate_logits(GA0, t, False)
                    if t < 2:
                        split(L, GA0 + t + 2, (GA0 + t) % 2)
                    else:
                        split(L, GA0 + t + 2, (GA0 + t) % 2, hid[:, 2 * t - 4:2 * t - 2, :])
                    dve.wait_ge(gate_th, L * 8 + 5 + t + CREDIT)
                    dve.scalar_tensor_tensor(out=gateth, in0=gateth, scalar=1.0, in1=hid[:, 8 + 2 * t:10 + 2 * t, :],
                                             op0=ALU.add, op1=ALU.mult)
                    dve.drain()
                    dve.scalar_tensor_tensor(out=hid[:, 2 * t:2 * t + 2, :], in0=hid[:, 2 * t:2 * t + 2, :], scalar=0.5,
                                             in1=gateth, op0=ALU.mult, op1=ALU.add).then_inc(m_ready, 1)
                    dve.drain()
                for t in range(3):
                    if t < 2:
                        split(L, WO0 + t + 2, (WO0 + t) % 2, hid[:, 2 * t + 4:2 * t + 6, :])
                    else:
                        split(L, F20, F20 % 2)
                post_norm(L, 1)
                update(L, 2)
                ffn(L, 1, F20, 2)
                post_norm(L, 2)
            for k in LAST_ORDER:
                due(DEPTH, 0, k)
                if k % 2 == 0:
                    dve.drain()
                    add(k)


def rope_tables():
    rot = HD // 4
    half = rot // 2
    inv = (np.float32(500000.0) ** (-np.arange(0, rot, 2, dtype=np.float32) / np.float32(rot))).astype(np.float32)
    ang = np.arange(T, dtype=np.float32)[None, :] * inv[:, None]
    cos, sin = np.cos(ang).astype(np.float32), np.sin(ang).astype(np.float32)
    C, S = np.ones((P, T), np.float32), np.zeros((P, T), np.float32)
    for base in (0, HD):
        C[base:base + half], C[base + half:base + rot] = cos, cos
        S[base:base + half], S[base + half:base + rot] = -sin, sin
    return C, S


def kernel(**inputs):
    import concourse.bacc as _bacc
    from concourse.bass_utils import run_bass_kernel_spmd as _run

    a = {k: np.asarray(v) for k, v in inputs.items()}
    C, S = rope_tables()
    init = [0.8 - 0.6 * math.exp(-0.3 * l) for l in range(DEPTH)]
    lam_const = np.broadcast_to(np.array(init + [1.0 - v for v in init], np.float32), (P, 2 * DEPTH))

    def columns(v):
        return v.reshape(-1, P).T

    arrays = {
        "xT": a["x"][0].T, "w_in": a["w_in"], "w_conv_out": a["w_conv_out"], "w_attn_out": a["w_attn_out"],
        "w_o": a["w_o"], "ffn1_w13": a["ffn1_w13"], "ffn1_w2": a["ffn1_w2"], "ffn2_w13": a["ffn2_w13"],
        "ffn2_w2": a["ffn2_w2"], "norm_wT": columns(a["norm_w"]), "b_gateT": columns(a["b_gate"]),
        "conv_wT": columns(a["conv_w"]), "sublnT": columns(a["subln_w"]), "lam_vec": a["lam_vec"],
        "ropeC": C, "ropeS": S, "ident_in": np.eye(P, dtype=np.float32), "lam_const": lam_const,
    }
    arrays = {f"in_{k}": np.ascontiguousarray(v) for k, v in arrays.items()}
    nc = _bacc.Bacc("TRN2", target_bir_lowering=False, num_devices=1)
    args = [nc.dram_tensor(k, v.shape, mybir.dt.from_np(v.dtype), kind="ExternalInput").ap() for k, v in arrays.items()]
    out = nc.dram_tensor("out_0", (D, T), mybir.dt.float32, kind="ExternalOutput").ap()
    encoder_kernel(nc, *args, out)
    r = _run(nc, [arrays], core_ids=[0])
    return np.ascontiguousarray(r.results[0]["out_0"].T)[None]
```
